# Optimizing a Trainium2 kernel written in Bass

```python
import jax, jax.numpy as jnp
from jax import lax
import numpy as np

D_MODEL = 1024
BATCH = 1
SEQ = 1024
DEPTH = 2

RET_HEADS = 4
RET_QK_DIM = 256
RET_V_DIM = 512
RET_CHUNK = 128
RET_IN = 2 * RET_HEADS * RET_QK_DIM + 2 * RET_HEADS * RET_V_DIM
ATT_Q_HEADS = 16
ATT_KV_HEADS = 4
ATT_GROUP = ATT_Q_HEADS // ATT_KV_HEADS
ATT_HEAD_DIM = 64
WINDOW = 128
ATT_IN = (ATT_Q_HEADS + 2 * ATT_KV_HEADS) * ATT_HEAD_DIM
D_FF = 4 * D_MODEL
N_MIXERS = 2
N_RET_LAYERS = (DEPTH + 1) // 2
N_ATT_LAYERS = DEPTH // 2
EPS = 1e-6
NEG_INF = -1e30

kernel_name = "hybrid_retention_swa_sink_alibi_encoder"

def rms_norm(x, g):
    xf = x.astype(jnp.float32)
    y = xf * lax.rsqrt(jnp.mean(xf * xf, axis=-1, keepdims=True) + EPS)
    return (y * g.astype(jnp.float32)).astype(x.dtype)

def retention_one_direction(q, k, v, log_gamma, strict):
    B, H, S, dk = q.shape
    dv = v.shape[-1]
    C = RET_CHUNK
    n = S // C
    lg = log_gamma.astype(jnp.float32)
    idx = jnp.arange(C, dtype=jnp.float32)
    diff = idx[:, None] - idx[None, :]
    mask = diff > 0 if strict else diff >= 0
    inner_decay = jnp.where(mask[None], jnp.exp(lg[:, None, None] * jnp.where(mask, diff, 0.0)[None]), 0.0)
    q_decay = jnp.exp(lg[:, None] * (idx + 1.0)[None])
    k_decay = jnp.exp(lg[:, None] * (C - 1.0 - idx)[None])
    chunk_decay = jnp.exp(lg * C)

    def to_chunks(a):
        return a.reshape(B, H, n, C, a.shape[-1]).transpose(2, 0, 1, 3, 4)

    def step(R, inp):
        qi, ki, vi = inp
        s = jnp.einsum('bhid,bhjd->bhij', qi, ki) * inner_decay
        inner = jnp.einsum('bhij,bhjv->bhiv', s, vi)
        cross = jnp.einsum('bhid,bhdv->bhiv', qi * q_decay[..., None], R)
        R_new = R * chunk_decay[:, None, None] + jnp.einsum('bhjd,bhjv->bhdv', ki * k_decay[..., None], vi)
        return R_new, inner + cross

    R0 = jnp.zeros((B, H, dk, dv), jnp.float32)
    _, out = lax.scan(step, R0, (to_chunks(q), to_chunks(k), to_chunks(v)))
    return out.transpose(1, 2, 0, 3, 4).reshape(B, H, S, dv)

def retention_mixer(h, w_in, w_out, log_decay_fwd, log_decay_bwd):
    B, S, _ = h.shape
    proj = h @ w_in
    nq = RET_HEADS * RET_QK_DIM
    nv = RET_HEADS * RET_V_DIM
    q, k, v, g = jnp.split(proj, [nq, 2 * nq, 2 * nq + nv], axis=-1)

    def heads(a, d):
        return a.reshape(B, S, RET_HEADS, d).transpose(0, 2, 1, 3).astype(jnp.float32)

    q = heads(q, RET_QK_DIM)
    k = heads(k, RET_QK_DIM) * (RET_QK_DIM ** -0.5)
    v = heads(v, RET_V_DIM)
    fwd = retention_one_direction(q, k, v, log_decay_fwd, strict=False)
    bwd = jnp.flip(retention_one_direction(jnp.flip(q, 2), jnp.flip(k, 2), jnp.flip(v, 2), log_decay_bwd, strict=True), 2)
    o = fwd + bwd
    o = o * lax.rsqrt(jnp.mean(o * o, axis=-1, keepdims=True) + EPS)
    o = o.transpose(0, 2, 1, 3).reshape(B, S, nv).astype(h.dtype)
    return (jax.nn.silu(g) * o) @ w_out

def alibi_slopes(n_heads):
    return jnp.exp2(-8.0 * jnp.arange(1, n_heads + 1, dtype=jnp.float32) / n_heads)

def windowed_gqa_mixer(h, w_in, w_out, sink):
    B, S, _ = h.shape
    W = WINDOW
    nb = S // W
    proj = h @ w_in
    nq = ATT_Q_HEADS * ATT_HEAD_DIM
    nk = ATT_KV_HEADS * ATT_HEAD_DIM
    q, k, v = jnp.split(proj, [nq, nq + nk], axis=-1)
    q = q.reshape(B, nb, W, ATT_KV_HEADS, ATT_GROUP, ATT_HEAD_DIM)

    def band(a):
        a = a.reshape(B, S, ATT_KV_HEADS, ATT_HEAD_DIM)
        a = jnp.pad(a, ((0, 0), (W, W), (0, 0), (0, 0))).reshape(B, nb + 2, W, ATT_KV_HEADS, ATT_HEAD_DIM)
        return jnp.concatenate([a[:, :-2], a[:, 1:-1], a[:, 2:]], axis=2)

    kb, vb = band(k), band(v)
    scores = jnp.einsum('bnqhgd,bnkhd->bnhgqk', q, kb).astype(jnp.float32) * (ATT_HEAD_DIM ** -0.5)
    i = jnp.arange(W)[:, None]
    j = jnp.arange(3 * W)[None, :]
    dist = jnp.abs(W + i - j)
    kpos = (jnp.arange(nb)[:, None] - 1) * W + jnp.arange(3 * W)[None, :]
    valid = (dist <= W)[None] & ((kpos >= 0) & (kpos < S))[:, None, :]
    slopes = alibi_slopes(ATT_Q_HEADS).reshape(ATT_KV_HEADS, ATT_GROUP)
    bias = -slopes[:, :, None, None] * dist.astype(jnp.float32)[None, None]
    scores = jnp.where(valid[None, :, None, None], scores + bias[None, None], NEG_INF)
    sink_col = jnp.broadcast_to(sink.astype(jnp.float32).reshape(ATT_KV_HEADS, ATT_GROUP)[None, None, :, :, None, None],
                                scores.shape[:-1] + (1,))
    probs = jax.nn.softmax(jnp.concatenate([scores, sink_col], axis=-1), axis=-1)[..., :-1]
    out = jnp.einsum('bnhgqk,bnkhd->bnqhgd', probs.astype(vb.dtype), vb)
    return out.reshape(B, S, nq) @ w_out

def squared_relu_mlp(h, w_up, w_down):
    a = jax.nn.relu(h @ w_up)
    return (a * a) @ w_down

def setup_inputs(seed: int = 0) -> dict:
    key = jax.random.key(seed)
    ks = jax.random.split(key, 16)
    f32 = jnp.float32

    def w(k, shape, fan_in):
        return jax.random.normal(k, shape, f32) * (fan_in ** -0.5)

    def gain(k):
        return 1.0 + 0.05 * jax.random.normal(k, (DEPTH, D_MODEL), f32)

    base = jnp.log1p(-jnp.exp2(-5.0 - jnp.arange(RET_HEADS, dtype=f32)))
    return {
        "x": jax.random.normal(ks[0], (BATCH, SEQ, D_MODEL), f32),
        "w_in_ret": w(ks[1], (N_RET_LAYERS, D_MODEL, RET_IN), D_MODEL),
        "w_out_ret": w(ks[2], (N_RET_LAYERS, RET_HEADS * RET_V_DIM, D_MODEL), RET_HEADS * RET_V_DIM),
        "log_decay_fwd": base[None] * (1.0 + 0.05 * jax.random.normal(ks[3], (N_RET_LAYERS, RET_HEADS), f32)),
        "log_decay_bwd": base[None] * (1.0 + 0.05 * jax.random.normal(ks[4], (N_RET_LAYERS, RET_HEADS), f32)),
        "w_in_attn": w(ks[5], (N_ATT_LAYERS, D_MODEL, ATT_IN), D_MODEL),
        "w_out_attn": w(ks[6], (N_ATT_LAYERS, ATT_Q_HEADS * ATT_HEAD_DIM, D_MODEL), ATT_Q_HEADS * ATT_HEAD_DIM),
        "sink_logits": 0.5 * jax.random.normal(ks[7], (N_ATT_LAYERS, ATT_Q_HEADS), f32),
        "g_pre_mix": gain(ks[8]),
        "g_post_mix": gain(ks[9]),
        "g_pre_mlp": gain(ks[10]),
        "g_post_mlp": gain(ks[11]),
        "w_up": w(ks[12], (DEPTH, D_MODEL, D_FF), D_MODEL),
        "w_down": w(ks[13], (DEPTH, D_FF, D_MODEL), D_FF),
    }

def reference(x, w_in_ret, w_out_ret, log_decay_fwd, log_decay_bwd, w_in_attn, w_out_attn,
              sink_logits, g_pre_mix, g_post_mix, g_pre_mlp, g_post_mlp, w_up, w_down):
    for layer in range(DEPTH):
        h = rms_norm(x, g_pre_mix[layer])
        if layer % N_MIXERS == 0:
            r = layer // N_MIXERS
            h = retention_mixer(h, w_in_ret[r], w_out_ret[r], log_decay_fwd[r], log_decay_bwd[r])
        else:
            a = layer // N_MIXERS
            h = windowed_gqa_mixer(h, w_in_attn[a], w_out_attn[a], sink_logits[a])
        x = x + rms_norm(h, g_post_mix[layer])
        h = squared_relu_mlp(rms_norm(x, g_pre_mlp[layer]), w_up[layer], w_down[layer])
        x = x + rms_norm(h, g_post_mlp[layer])
    return x


_drawn_inputs = setup_inputs


def setup_inputs(seed=0):
    import zlib

    import numpy as np

    out = dict(_drawn_inputs(seed))
    spreads = {}
    factors = {'sink_logits': 7.537}
    for name, (base, spread) in spreads.items():
        noise = np.random.default_rng([zlib.crc32(name.encode()), seed]).standard_normal(out[name].shape)
        drawn = base * np.exp(spread * noise) if base else spread * noise
        out[name] = __import__('jax').numpy.asarray(drawn.astype(out[name].dtype))
    for name, factor in factors.items():
        out[name] = (out[name] * factor).astype(out[name].dtype)
    return out
```

```python
import concourse.bass as bass
from concourse import mybir

P = 128
D = 1024
T = 1024
KT = D // P
TB = T // P
HALF = 512
RH, DK, DV = 4, 256, 512
NQ, NV = RH * DK, RH * DV
AH, AG, HD = 16, 4, 64
FF = 4 * D
EPS = 1e-6
BIG = 1e30

RAW = 2
WS = 4
UNIT = 1024
CR = 4

R_UNITS, R_PROJ, R_SCORE, R_OUT = 16, 24, 18, 8
G_UNITS, G_OUT = 4, 16
TAIL = 24
M_PROJ = 4
A_UNITS, A_CORE, A_SCORE = 6, 16, 64
A_BLOCKS = [[kb for kb in (b - 1, b, b + 1) if 0 <= kb < TB] for b in range(TB)]
A_PT = 2 * sum(len(x) for x in A_BLOCKS)
A_PROJ = 18 + A_PT
N_O0, N_O1, N_M = NV // (2 * P), D // (2 * P), FF // (2 * P)


def bases():
    unit = proj = score = out = ff = 0
    b = {}

    def at(name):
        b[name] = (unit, proj, score, out, ff)
    at("E0"); score += 16
    at("R"); unit += RH * R_UNITS; proj += RH * R_PROJ; score += RH * R_SCORE; out += RH * R_OUT
    at("O0"); unit += N_O0 * G_UNITS; out += (N_O0 - 2) * G_OUT + TAIL
    at("E1"); score += 16
    at("M0"); unit += N_M * G_UNITS; proj += N_M * M_PROJ; out += (N_M - 2) * G_OUT + TAIL; ff += N_M * M_PROJ
    at("E2"); score += 16
    at("A"); unit += 2 * A_UNITS; proj += 2 * A_PROJ; score += 2 * A_SCORE
    at("O1"); unit += N_O1 * G_UNITS; out += (N_O1 - 2) * G_OUT + TAIL
    at("E3"); score += 16
    at("M1"); unit += N_M * G_UNITS; proj += N_M * M_PROJ; out += (N_M - 2) * G_OUT + TAIL; ff += N_M * M_PROJ
    at("E4")
    return b


BASE = bases()


class Steps:

    def __init__(self, eng, sem):
        self.eng, self.sem, self.n, self.base = eng, sem, 0, 0

    def __call__(self, ins):
        ins.then_inc(self.sem, 1)
        self.n += 1
        self.eng.wait_ge(self.sem, self.base + self.n)

    def enter(self, i, stride):
        self.start, self.stride, self.base = self.n, stride, i * stride

    def leave(self, rounds):
        assert self.n - self.start == self.stride, (self.n - self.start, self.stride)
        self.n, self.base = self.start + rounds * self.stride, 0


def build(nc, x, w_in_ret, w_out_ret, log_decay_fwd, log_decay_bwd, w_in_attn, w_out_attn, sink_logits,
          g_pre_mix, g_post_mix, g_pre_mlp, g_post_mlp, w_up, w_down, out):
    f32, f32r, f16, i32 = mybir.dt.float32, mybir.dt.float32r, mybir.dt.float16, mybir.dt.int32
    ACT, ALU, AX = mybir.ActivationFunctionType, mybir.AluOpType, mybir.AxisListType

    at = [(nc.sbuf_base + 63) // 64 * 64]

    def sb(name, shape, dt, offset=None):
        size = 4
        for s in shape[1:]:
            size *= s
        size = (size // 2 if dt == f16 else size) + 31 & -32
        if offset is None:
            offset, at[0] = at[0], at[0] + size
        assert offset + size <= nc.sbuf_usable_end, (name, offset + size, nc.sbuf_usable_end)
        return nc.alloc_sbuf_tensor_at(name, shape, dt, offset=offset)

    hT = [sb("hT_hi", [P, KT, T], f32r), sb("hT_lo", [P, KT, T], f32r)]
    w_raw = sb("w_raw", [P, RAW, UNIT], f32)
    w_split = [sb("w_hi", [P, WS, UNIT], f32r), sb("w_lo", [P, WS, UNIT], f32r)]
    ident = sb("ident", [P, P], f32)
    ones = sb("ones", [P, P], f32)
    one = ones[:, 0:1]
    stats = sb("stats", [P, 6, TB], f32)
    eps_t = sb("eps_t", [P, 1], f32)
    decay = sb("decay", [P, 2, RH], f32)
    decay_now = sb("decay_now", [P, 2], f32)
    slope = sb("slope", [P, AH], f32)
    slope_now = sb("slope_now", [P, 8], f32)
    sink = sb("sink", [P, AH], f32)
    sink_now = sb("sink_now", [P, 8], f32)
    smax = sb("smax", [P, 2, 4], f32)
    nmax = sb("nmax", [P, 2, 4], f32)
    sink_gap = sb("sink_gap", [P, 2, 4], f32)
    sink_exp = sb("sink_exp", [P, 2, 4], f32)
    row_sum = sb("row_sum", [P, 2, 4], f32)
    row_inv = sb("row_inv", [P, 2, 4], f32)
    a_iota = sb("a_iota", [P, 3 * P], i32)
    arena = (at[0] + 63) // 64 * 64

    at[0] = arena
    r_qT = [sb("r_qT_hi", [P, 2, T], f32r), sb("r_qT_lo", [P, 2, T], f32r)]
    r_kT = [sb("r_kT_hi", [P, 2, T], f32r), sb("r_kT_lo", [P, 2, T], f32r)]
    r_v = [sb("r_v_hi", [P, TB, DV], f32r), sb("r_v_lo", [P, TB, DV], f32r)]
    MASK = 2 * T - P
    dist16 = sb("dist16", [P, MASK], f16)
    r_aT = [sb("r_aT_hi", [P, 2, HALF], f32r), sb("r_aT_lo", [P, 2, HALF], f32r)]
    mask = sb("mask", [P, MASK], f32)
    r_am = sb("r_am", [P, 2, HALF], f32)
    r_os = sb("r_os", [P, 4, HALF], f32)
    r_e = sb("r_e", [P, HALF], f32)
    r_sd = sb("r_sd", [P, HALF], f32)

    dist_i = sb("dist_i", [P, MASK], i32, offset=arena)

    at[0] = arena
    aT = [sb("aT_hi", [P, 2, 2, T], f32r), sb("aT_lo", [P, 2, 2, T], f32r)]
    y = sb("y", [P, TB, D], f32)
    relu = sb("relu", [P, 2, HALF], f32)
    relu_sq = sb("relu_sq", [P, 2, HALF], f32)
    squares = relu_sq[:, :, :].rearrange("p a t -> p (a t)")
    xt = sb("xt", [P, 3, D], f32)
    xn = sb("xn", [P, 2, D], f32)
    gain_post = sb("gain_post", [P, D], f32)
    gain_pre = sb("gain_pre", [P, D], f32)

    at[0] = arena
    a_qT = [sb("a_qT_hi", [P, 4, T], f32r), sb("a_qT_lo", [P, 4, T], f32r)]
    a_kT = [sb("a_kT_hi", [P, T], f32r), sb("a_kT_lo", [P, T], f32r)]
    a_v = [sb("a_v_hi", [P, TB, P], f32r), sb("a_v_lo", [P, TB, P], f32r)]
    a_pT = [sb("a_pT_hi", [P, 4, HALF], f32r), sb("a_pT_lo", [P, 4, HALF], f32r)]
    a_s = sb("a_s", [P, 4, 4, 3 * P], f32)
    a_out = sb("a_out", [P, 2, HALF], f32)
    a_dist = sb("a_dist", [P, 3 * P], f32)
    a_far = sb("a_far", [P, 3 * P], f32)

    banks = [nc.alloc_psum_tensor(f"bank{i}", [P, HALF], f32) for i in range(8)]
    score_bank, proj_bank, out_bank = banks[0:2], banks[2:4], banks[4:8]

    mix = nc.dram_tensor("mix", (NV, T), f32).ap()
    x_mid = [nc.dram_tensor(f"x_mid{i}", (T, D), f32).ap() for i in range(3)]
    x_in = [x[0], x[0], x_mid[0], x_mid[1], x_mid[2]]
    x_out = [None, x_mid[0], x_mid[1], x_mid[2], out[0]]
    post = [None, g_post_mix[0], g_post_mlp[0], g_post_mix[1], g_post_mlp[1]]
    pre = [g_pre_mix[0], g_pre_mlp[0], g_pre_mix[1], g_pre_mlp[1], None]

    sem = nc.alloc_semaphore
    raw_loaded = [sem(f"raw_loaded{i}") for i in range(RAW)]
    unit_hi = sem("unit_hi")
    unit_split = sem("unit_split")
    proj_done, proj_free = sem("proj_done"), sem("proj_free")
    score_done, score_free = sem("score_done"), sem("score_free")
    out_done, out_free = sem("out_done"), sem("out_free")
    proj_hi = sem("proj_hi")
    consts = sem("consts")
    params = sem("params")
    act_step, dve_step = sem("act_step"), sem("dve_step")
    gains_loaded = sem("gains_loaded")
    x_loaded = [sem(f"x_loaded{i}") for i in range(3)]
    x_stored = [sem(f"x_stored{i}") for i in range(3)]
    std_y, std_x = sem("std_y"), sem("std_x")
    z_ready = sem("z_ready")
    x_new = sem("x_new")
    xn_ready = sem("xn_ready")
    hT_hi_ready = sem("hT_hi_ready")
    sq_ready = sem("sq_ready")
    ff_hi = sem("ff_hi")
    ff_ready = sem("ff_ready")
    mask_ready = sem("mask_ready")
    mask_exp = sem("mask_exp")
    aT_hi_ready = sem("aT_hi_ready")
    aT_ready = sem("aT_ready")
    pv_done = sem("pv_done")
    sq_out = sem("sq_out")
    sq_sum = sem("sq_sum")
    e_ready = sem("e_ready")
    gated = sem("gated")
    mix_stored = [sem(f"mix_stored{i}") for i in range(4)]
    max_ready = sem("max_ready")
    exp_ready = sem("exp_ready")
    inv_ready = sem("inv_ready")
    p_ready = sem("p_ready")
    attn_done, attn_free = sem("attn_done"), sem("attn_free")
    attn_out = [sem(f"attn_out{i}") for i in range(2)]
    credited = [unit_split, proj_done, proj_free, score_done, score_free, out_done, out_free,
                aT_hi_ready, aT_ready, pv_done, attn_done, attn_free, p_ready, sq_ready]

    def part(k, n=P):
        return slice(k * n, (k + 1) * n)

    def cut(pair, *idx):
        return [t[(slice(None), *idx)] for t in pair]

    def wslot(s, cols):
        return cut(w_split, s, cols)

    ATTN_STORES = 16 * (1 + A_CORE)

    block = nc.Block()
    with block:

        @block.sync
        def _(sp):
            for s in credited:
                sp.sem_inc(s, CR)
            for s in mix_stored + attn_out:
                sp.sem_inc(s, 16)

            def load(n, slot, dst, src):
                sp.wait_ge(unit_split, CR + n - RAW + 1)
                sp.dma_start(dst, src).then_inc(raw_loaded[slot], 16)

            def by_column(slot):
                return w_raw[:, slot, :].rearrange("p (k c) -> p k c", k=KT)

            w_r = w_in_ret[0].rearrange("(k p) c -> p k c", p=P)
            with sp.Fori(0, RH) as h:
                n = h * R_UNITS
                idx = 0
                for c0 in (0, NQ):
                    for u in range(2):
                        load(n + idx, idx % RAW, by_column(idx % RAW), w_r[:, :, bass.ds(h * DK + (c0 + u * P), P)])
                        idx += 1
                for u in range(4):
                    load(n + idx, idx % RAW, w_raw[:, idx % RAW, :].rearrange("p (k c) -> p k c", k=2),
                         w_r[:, 2 * u:2 * u + 2, bass.ds(h * DV + 2 * NQ, DV)])
                    idx += 1
                for th in range(2):
                    for u in range(4):
                        load(n + idx, idx % RAW, by_column(idx % RAW),
                             w_r[:, :, bass.ds(h * DV + (2 * NQ + NV + u * P), P)])
                        idx += 1

            def load_outputs(phase, groups, w, stored, each):
                n0 = BASE[phase][0]
                with sp.Fori(0, groups // 2) as i:
                    stores = sp.snap(i * each + (16 + each))
                    slot_free = sp.snap(i * (2 * G_UNITS) + (n0 + CR - RAW + 1))
                    for st in stored:
                        sp.wait_ge(st, stores)
                    sp.wait_ge(unit_split, slot_free)
                    for par in range(2):
                        n, row = i * (2 * G_UNITS) + (n0 + G_UNITS * par), i * (4 * P) + 2 * P * par
                        for u in range(2):
                            load(n + u, u, w_raw[:, u, :], mix[bass.ds(row + u * P, P), :])
                        for u in range(2):
                            load(n + (2 + u), u, w_raw[:, u, :], w[bass.ds(row + u * P, P), :])

            def load_mlp(phase, layer):
                n0 = BASE[phase][0]
                up = w_up[layer].rearrange("(k p) c -> p k c", p=P)
                down = w_down[layer]
                for u in range(2):
                    load(n0 + u, u, by_column(u), up[:, :, part(u)])
                with sp.Fori(0, N_M - 1) as g:
                    for u in range(2):
                        load(g * G_UNITS + (n0 + 2 + u), u, by_column(u), up[:, :, bass.ds(g * (2 * P) + (2 + u) * P, P)])
                    for u in range(2):
                        load(g * G_UNITS + (n0 + 4 + u), u, w_raw[:, u, :], down[bass.ds(g * (2 * P) + u * P, P), :])
                for u in range(2):
                    load(n0 + (N_M - 1) * G_UNITS + 2 + u, u, w_raw[:, u, :], down[part(2 * (N_M - 1) + u), :])

            load_outputs("O0", N_O0, w_out_ret[0], mix_stored, 16 * 2)
            load_mlp("M0", 0)

            wa = w_in_attn[0].rearrange("(k p) c -> p k c", p=P)
            n0 = BASE["A"][0]
            with sp.Fori(0, 2) as gp:
                n = gp * A_UNITS + n0
                for j in range(4):
                    s = j % RAW
                    sp.wait_ge(unit_split, n + (CR + j - RAW + 1))
                    for two in range(2):
                        dst = w_raw[:, s, :].rearrange("p (k two c) -> p k two c", k=KT, two=2)[:, :, two, :]
                        sp.dma_start(dst, wa[:, :, bass.ds(gp * (8 * HD) + (4 * two + j) * HD, HD)]) \
                          .then_inc(raw_loaded[s], 16)
                for u in range(2):
                    load(n + (4 + u), u, by_column(u), wa[:, :, bass.ds(gp * P + (AH * HD + u * AG * HD), P)])

            load_outputs("O1", N_O1, w_out_attn[0], attn_out, 16 * A_CORE // 2)
            load_mlp("M1", 1)

        @block.gpsimd
        def _(pool):
            pool.memset(ident[:, :], 0.0).then_inc(consts, 1)
            pool.wait_ge(consts, 1)
            pool.affine_select(out=ident[:, :], in_=ident[:, :], compare_op=ALU.not_equal, fill=1.0, base=0,
                               pattern=[[-1, P]], channel_multiplier=1).then_inc(consts, 1)
            pool.memset(ones[:, :], 1.0).then_inc(consts, 1)
            pool.memset(eps_t[:, :], EPS).then_inc(consts, 1)
            for i in range(AH):
                pool.memset(slope[:, i:i + 1], -2.0 ** (-8.0 * (i + 1) / AH)).then_inc(consts, 1)
            pool.iota(dist_i[:, :], pattern=[[1, MASK]], base=-(T - P), channel_multiplier=-1).then_inc(consts, 1)
            pool.iota(a_iota[:, :], pattern=[[1, 3 * P]], base=-P, channel_multiplier=-1).then_inc(consts, 1)
            pool.wait_ge(consts, 6 + AH)

            def cut_unit(slot, loaded, dst, n):
                pool.wait_ge(raw_loaded[slot], loaded)
                raw = w_raw[:, slot, :]
                pool.tensor_tensor(dst[0], raw, one.broadcast_to([P, UNIT]), ALU.mult).then_inc(unit_hi, 1)
                pool.wait_ge(unit_hi, n + 1)
                pool.tensor_tensor(dst[1], raw, dst[0].bitcast(f32), ALU.subtract).then_inc(unit_split, 1)

            with pool.Fori(0, RH) as h:
                for i in range(R_UNITS):
                    free_at = {0: -3, 1: -2, 2: -1, 3: 0, 4: 2, 5: 4, 6: 6, 7: 8}.get(i, 16 if i < 12 else 17 + i - 12)
                    pool.wait_ge(proj_done, h * R_PROJ + (CR + free_at))
                    cut_unit(i % RAW, h * (16 * R_UNITS // RAW) + 16 * (i // RAW + 1), wslot(i % WS, slice(None)),
                             h * R_UNITS + i)
            loaded0 = 16 * (RH * R_UNITS // RAW)

            def cut_outputs(phase, groups, loaded0, first_waits):
                n0, _, _, o0, _ = BASE[phase]

                def pair(i, waits):
                    for par in range(2):
                        for u in range(4):
                            if waits is None:
                                pool.wait_ge(out_done, i * (2 * G_OUT) + (CR + o0 + G_OUT * (par - 1)))
                            else:
                                pool.wait_ge(*waits[par][u])
                            dst = cut(aT, par, u) if u < 2 else wslot(2 * par + u - 2, slice(None))
                            cut_unit(u % RAW, i * 64 + (loaded0 + 32 * par + 16 * (u // RAW + 1)), dst,
                                     i * (2 * G_UNITS) + (n0 + G_UNITS * par + u))
                pair(0, first_waits)
                with pool.Fori(1, groups // 2) as i:
                    pair(i, None)
                return loaded0 + 16 * (groups * G_UNITS // RAW)

            def add_residual(e, between):
                for tb in range(TB):
                    s = tb % 3
                    pool.wait_ge(x_loaded[s], 16 * (e * (3, 3, 2)[s] + tb // 3 + 1))
                    pool.wait_ge(z_ready, (e - 1) * TB + tb + 1)
                    pool.tensor_tensor(xt[:, s, :], xt[:, s, :], y[:, tb, :], ALU.add).then_inc(x_new, 1)
                    if tb in between:
                        between[tb]()

            def cut_mlp(phase, e, loaded0):
                n0, p0, _, o0, _ = BASE[phase]

                def first(u):
                    pool.wait_ge(out_done, CR + o0 - 8)
                    cut_unit(u, loaded0 + 16, wslot(u, slice(None)), n0 + u)
                add_residual(e, {3: lambda: first(0), 5: lambda: first(1)})
                pool.wait_ge(out_done, CR + o0)
                for u in range(2):
                    cut_unit(u, loaded0 + 32, wslot(2 + u, slice(None)), n0 + 2 + u)
                pool.wait_ge(proj_done, CR + p0 + M_PROJ)
                for u in range(2):
                    cut_unit(u, loaded0 + 48, wslot(u, slice(None)), n0 + 4 + u)
                with pool.Fori(1, N_M - 1) as g:
                    for u in range(2):
                        pool.wait_ge(proj_done, g * M_PROJ + (CR + p0 + 3 + u))
                        cut_unit(u, g * 32 + (loaded0 + 32), wslot(2 + u, slice(None)), g * G_UNITS + (n0 + 2 + u))
                    for u in range(2):
                        pool.wait_ge(out_done, g * G_OUT + (CR + o0))
                        cut_unit(u, g * 32 + (loaded0 + 48), wslot(u, slice(None)), g * G_UNITS + (n0 + 4 + u))
                g = N_M - 1
                for u in range(2):
                    pool.wait_ge(proj_done, CR + p0 + g * M_PROJ + 3 + u)
                    cut_unit(u, loaded0 + 32 + 32 * g, wslot(2 + u, slice(None)), n0 + 2 + g * G_UNITS + u)
                return loaded0 + 16 * (N_M * G_UNITS // RAW)

            p_end = CR + RH * R_PROJ
            scores_read = (score_done, CR + BASE["R"][2] + RH * R_SCORE - 1)
            loaded0 = cut_outputs("O0", N_O0, loaded0, [
                [scores_read, scores_read, (proj_done, p_end - 3), (proj_done, p_end - 2)],
                [scores_read, scores_read, (proj_done, p_end - 1), (proj_done, p_end)]])
            loaded0 = cut_mlp("M0", 1, loaded0)

            n0, p0, s0, o0, _ = BASE["A"]

            def cut_q(gp, j):
                if gp:
                    pool.wait_ge(proj_done, CR + p0 + 18)
                else:
                    pool.wait_ge(out_done, CR + o0 - 8 * (j < 2))
                cut_unit(j % RAW, loaded0 + 80 * gp + 32 * (j // RAW + 1), wslot(j, slice(None)), n0 + gp * A_UNITS + j)
            add_residual(2, {3: lambda: cut_q(0, 0), 5: lambda: cut_q(0, 1)})
            for gp in range(2):
                if gp == 0:
                    cut_q(0, 2)
                    cut_q(0, 3)
                for u in range(2):
                    pool.wait_ge(proj_done, CR + p0 + gp * A_PROJ + 2 * (u + 1))
                    cut_unit(u, loaded0 + 80 * gp + 80, wslot(u, slice(None)), n0 + gp * A_UNITS + 4 + u)
                for c in range(A_CORE):
                    nk = len(A_BLOCKS[c // 2]) * P
                    pool.wait_ge(inv_ready, gp * A_CORE + c + 1)
                    s = a_s[:, c % 4, :, 0:nk]
                    pool.tensor_tensor(s, s, row_inv[:, c % 2, :].unsqueeze(2).broadcast_to([P, 4, nk]), ALU.mult) \
                        .then_inc(p_ready, 1)
                    if gp == 0 and c in (2, 5, 8, 11):
                        cut_q(1, (c - 2) // 3)
            loaded0 += 160
            p_end = CR + p0 + 2 * A_PROJ - A_PT
            scores_read = (score_done, CR + s0 + 2 * A_SCORE)
            loaded0 = cut_outputs("O1", N_O1, loaded0, [
                [scores_read, scores_read, (proj_done, p_end), (proj_done, p_end)]] * 2)
            loaded0 = cut_mlp("M1", 3, loaded0)
            add_residual(4, {})

        @block.tensor
        def _(pe):
            def mm3(dst, stat, mov, first, last):
                pe.matmul(dst, stat[0], mov[0], start=first, stop=False)
                pe.matmul(dst, stat[0], mov[1], start=False, stop=False)
                return pe.matmul(dst, stat[1], mov[0], start=False, stop=last)

            def unit_ready(n):
                pe.wait_ge(unit_split, n + (CR + 1))

            def transpose_norm(phase, tb):
                s0 = BASE[phase][2]
                pe.wait_ge(xn_ready, int(phase[1]) * TB + tb + 1)
                for j in range(2):
                    pe.wait_ge(score_free, CR + s0 + 2 * tb + j - 1)
                    for k in range(4):
                        mm = pe.transpose(score_bank[j][:, part(k)], xn[:, tb % 2, part(4 * j + k)], ident[:, :])
                    mm.then_inc(score_done, 1)

            def hT_ready(phase, halves):
                pe.wait_ge(score_free, CR + BASE[phase][2] + 8 * halves)

            def project(slot, th, bank, free):
                pe.wait_ge(proj_free, free)
                for k in range(KT):
                    mm = mm3(proj_bank[bank][:, :], wslot(slot, part(k)), cut(hT, k, part(th, HALF)), k == 0, k == KT - 1)
                mm.then_inc(proj_done, 1)

            pe.wait_ge(consts, 6 + AH)
            for tb in range(TB):
                transpose_norm("E0", tb)
            hT_ready("E0", 2)

            _, p0, s0, o0, _ = BASE["R"]
            with pe.Fori(0, RH) as h:
                n, pj, sj = h * R_UNITS, h * R_PROJ + (CR + p0), h * R_SCORE + (CR + s0)
                for i in range(4):
                    unit_ready(n + i)
                    for th in range(2):
                        project(i, th, th, pj + (2 * i + th - 1))
                for b in range(TB):
                    pe.wait_ge(proj_free, pj + (8 + b - 1))
                    for k in range(KT):
                        if b == 0 and k % 2 == 0:
                            unit_ready(n + (4 + k // 2))
                        mm = mm3(proj_bank[b % 2][:, :], cut(hT, k, part(b)), wslot(k // 2, part(k % 2, HALF)),
                                 k == 0, k == KT - 1)
                    mm.then_inc(proj_done, 1)
                for th in range(2):
                    def scores(b):
                        j = 9 * th + b
                        if th == 0 and b == 0:
                            pe.wait_ge(proj_free, pj + 8)
                        pe.wait_ge(score_free, sj + (j - 1))
                        for k in range(2):
                            mm = mm3(score_bank[j % 2][:, :], cut(r_kT, k, part(b)), cut(r_qT, k, part(th, HALF)),
                                     k == 0, k == 1)
                        mm.then_inc(score_done, 1)

                    def values(b):
                        if th == 0 and b == 0:
                            pe.wait_ge(proj_free, pj + 16)
                        pe.wait_ge(aT_ready, h * 16 + (CR + 8 * th + b + 1))
                        for dt in range(4):
                            if b == 0:
                                pe.wait_ge(out_free, h * 8 + (CR + o0 + 4 * th + dt - 3))
                            mm = mm3(out_bank[dt][:, :], cut(r_v, b, part(dt)), cut(r_aT, b % 2), b == 0, b == TB - 1)
                            if b == TB - 1:
                                mm.then_inc(out_done, 1)
                        if b < TB - 1:
                            mm.then_inc(pv_done, 1)
                    scores(0)
                    for b in range(TB):
                        if b + 1 < TB:
                            scores(b + 1)
                        values(b)

                    def gate(dt):
                        i = 8 + 4 * th + dt
                        unit_ready(n + i)
                        project(i % WS, th, dt % 2, pj + (16 + 4 * th + dt - 1))
                    gate(0)
                    j = 9 * th + 8
                    pe.wait_ge(sq_sum, h * 2 + (th + 1))
                    pe.wait_ge(score_free, sj + (j - 1))
                    pe.matmul(score_bank[j % 2][:, :], ones[:, :], r_am[:, 0, :], start=True, stop=True) \
                      .then_inc(score_done, 1)
                    for dt in range(1, 4):
                        gate(dt)

            def out_tiles(parts, first_job, j, tb):
                for dh in range(2):
                    pe.wait_ge(out_free, first_job + (j + dh - 3))
                    for i, (par, slot) in enumerate(parts):
                        for k in range(2):
                            mm = mm3(out_bank[(j + dh) % 4][:, :], cut(aT, par, k, part(tb)),
                                     wslot(slot + k, part(dh, HALF)), i + k == 0, k == 1 and i == len(parts) - 1)
                    mm.then_inc(out_done, 1)

            def out_group(par, slot, first_job):
                for tb in range(TB):
                    out_tiles([(par, slot)], first_job, 2 * tb, tb)

            def tail(phase, first_job, last_ready, hidden=None):
                more = phase != "E4"
                for tb in range(4, TB):
                    out_tiles([(0, 0)], first_job, 2 * (tb - 4), tb)
                last_ready()
                for tb in range(TB):
                    out_tiles([(0, 0), (1, 2)] if tb < 4 else [(1, 2)], first_job, 8 + 2 * tb, tb)
                    if more and tb >= 3:
                        transpose_norm(phase, tb - 3)
                if more:
                    if hidden:
                        hT_ready(phase, 1)
                        hidden(0)
                    transpose_norm(phase, TB - 3)
                    if hidden:
                        hidden(1)
                    transpose_norm(phase, TB - 2)
                    transpose_norm(phase, TB - 1)

            def outputs(phase, groups, after, hidden):
                n0, _, _, o0, _ = BASE[phase]
                with pe.Fori(0, groups // 2 - 1) as i:
                    for par in range(2):
                        unit_ready(i * (2 * G_UNITS) + (n0 + G_UNITS * par + 3))
                        out_group(par, 2 * par, i * (2 * G_OUT) + (CR + o0 + G_OUT * par))
                unit_ready(n0 + G_UNITS * (groups - 2) + 3)
                tail(after, CR + o0 + G_OUT * (groups - 2), lambda: unit_ready(n0 + G_UNITS * (groups - 1) + 3), hidden)

            def first_hidden(phase):
                n0, p0 = BASE[phase][:2]

                def job(u):
                    unit_ready(n0 + u)
                    project(u, 0, u, CR + p0 + u - 1)
                return job

            def mlp(phase, before, after):
                n0, p0, _, o0, f0 = BASE[phase]

                def up(g, slot, unit, halves=(0, 1)):
                    for th in halves:
                        for u in range(2):
                            if th == 0:
                                unit_ready(unit + u)
                            project(slot + u, th, u, g * M_PROJ + (CR + p0 + 2 * th + u - 1))

                def ready(g, unit):
                    unit_ready(unit)
                    pe.wait_ge(ff_ready, g * M_PROJ + (f0 + M_PROJ))
                up(0, 0, n0, halves=(1,))
                with pe.Fori(0, N_M // 2 - 1) as i:
                    for par in range(2):
                        g = i * 2 + par
                        up(g + 1, 2, g * G_UNITS + (n0 + 2))
                        ready(g, g * G_UNITS + (n0 + 5))
                        out_group(par, 0, g * G_OUT + (CR + o0))
                g = N_M - 2
                up(g + 1, 2, n0 + 2 + g * G_UNITS)
                ready(g, n0 + 5 + g * G_UNITS)
                tail(after, CR + o0 + g * G_OUT, lambda: ready(g + 1, n0 + 3 + (g + 1) * G_UNITS))

            outputs("O0", N_O0, "E1", first_hidden("M0"))
            hT_ready("E1", 2)
            mlp("M0", "E1", "E2")
            hT_ready("E2", 2)

            n0, p0, s0, _, _ = BASE["A"]
            with pe.Fori(0, 2) as gp:
                n, pj, sj = gp * A_UNITS + n0, gp * A_PROJ + (CR + p0), gp * A_SCORE + (CR + s0)
                for i in range(5):
                    unit_ready(n + i)
                    for th in range(2):
                        project(i % WS, th, th, pj + (2 * i + th - 1))
                unit_ready(n + 5)
                for b in range(TB):
                    pe.wait_ge(proj_free, pj + (10 + b - 1))
                    for k in range(KT):
                        mm = mm3(proj_bank[b % 2][:, 0:P], cut(hT, k, part(b)), wslot(1, part(k)), k == 0, k == KT - 1)
                    mm.then_inc(proj_done, 1)
                pe.wait_ge(proj_free, pj + 18)
                done = 0
                for step in range(A_CORE + 3):
                    c = step - 3
                    if c >= 0:
                        pe.wait_ge(p_ready, gp * A_CORE + (CR + c + 1))
                        first = done
                        for i in range(len(A_BLOCKS[c // 2])):
                            j = 18 + done
                            pe.wait_ge(proj_free, pj + (j - 1))
                            for head in range(4):
                                mm = pe.transpose(proj_bank[j % 2][:, part(head)], a_s[:, c % 4, head, part(i)],
                                                  ident[:, :])
                            mm.then_inc(proj_done, 1)
                            done += 1
                    if step < A_CORE:
                        b, two = step // 2, step % 2
                        blocks = A_BLOCKS[b]
                        rows = slice(HD * two, HD * two + HD)
                        for head in range(4):
                            pe.wait_ge(score_free, sj + (4 * step + head - 1))
                            q = [t[rows, head, part(b)] for t in a_qT]
                            k = [t[rows, blocks[0] * P:(blocks[-1] + 1) * P] for t in a_kT]
                            mm3(score_bank[head % 2][:, 0:len(blocks) * P], q, k, True, True).then_inc(score_done, 1)
                    if c >= 0:
                        pe.wait_ge(attn_free, gp * A_CORE + (CR + c - 3))
                        blocks = A_BLOCKS[c // 2]
                        for i, kb in enumerate(blocks):
                            pe.wait_ge(proj_free, pj + (18 + first + i + 1))
                            mm3(out_bank[c % 4][:, :], cut(a_v, kb, slice(None)), cut(a_pT, (first + i) % 4),
                                i == 0, i == len(blocks) - 1).then_inc(attn_done, 1)

            pe.wait_ge(attn_free, CR + 2 * A_CORE)
            outputs("O1", N_O1, "E3", first_hidden("M1"))
            hT_ready("E3", 2)
            mlp("M1", "E3", "E4")

        @block.scalar
        def _(act):
            step = Steps(act, act_step)
            x_loads, x_stores = [0] * 3, [0] * 3

            act.dma_start(decay[:, 0, :], log_decay_fwd[0].partition_broadcast(P)).then_inc(params, 16)
            act.dma_start(decay[:, 1, :], log_decay_bwd[0].partition_broadcast(P)).then_inc(params, 16)
            act.dma_start(sink[:, :], sink_logits[0].partition_broadcast(P)).then_inc(params, 16)

            def load_x(e, tb):
                s = tb % 3
                if x_stores[s]:
                    act.wait_ge(x_stored[s], 16 * x_stores[s])
                act.dma_start(xt[:, s, :], x_in[e][part(tb), :]).then_inc(x_loaded[s], 16)
                x_loads[s] += 1

            def norm(e):
                phase = f"E{e}"
                s0, o0 = BASE[phase][2], BASE[phase][3]
                for i, g in enumerate((post[e], pre[e])):
                    if g is not None:
                        act.dma_start((gain_post, gain_pre)[i][:, :], g.partition_broadcast(P)).then_inc(gains_loaded, 16)
                load_x(e, 0)
                load_x(e, 1)
                for st in range(TB + 3):
                    tb = st
                    if e and tb < TB:
                        act.wait_ge(out_free, CR + o0 - 16 + 2 * (tb + 1))
                        step(act.activation(squares, y[:, tb, :], ACT.Square, scale=D ** -0.5,
                                            accum_out=stats[:, 0, tb:tb + 1]))
                        act.activation(stats[:, 1, tb:tb + 1], stats[:, 0, tb:tb + 1], ACT.Sqrt, bias=eps_t[:, :]) \
                           .then_inc(std_y, 1)
                    tb = st - 3
                    if e < 4 and 0 <= tb < TB:
                        for j in range(2):
                            act.wait_ge(score_done, CR + s0 + 2 * tb + j + 1)
                            act.activation(hT[0][:, 4 * j:4 * j + 4, part(tb)],
                                           score_bank[j][:, :].rearrange("p (k t) -> p k t", k=4), ACT.Copy) \
                               .then_inc(hT_hi_ready, 1)
                    tb = st - 1
                    if 0 <= tb < TB:
                        if e:
                            act.wait_ge(x_new, (e - 1) * TB + tb + 1)
                            act.dma_start(x_out[e][part(tb), :], xt[:, tb % 3, :]).then_inc(x_stored[tb % 3], 16)
                            x_stores[tb % 3] += 1
                        else:
                            act.wait_ge(x_loaded[tb % 3], 16 * (tb // 3 + 1))
                            if tb == 0:
                                act.wait_ge(consts, 6 + AH)
                        if e < 4:
                            step(act.activation(squares, xt[:, tb % 3, :], ACT.Square, scale=D ** -0.5,
                                                accum_out=stats[:, 2, tb:tb + 1]))
                            act.activation(stats[:, 3, tb:tb + 1], stats[:, 2, tb:tb + 1], ACT.Sqrt, bias=eps_t[:, :]) \
                               .then_inc(std_x, 1)
                    if 1 <= st < TB - 1:
                        if e < 4 and st >= 2:
                            act.wait_ge(xn_ready, e * TB + st - 1)
                        load_x(e, st + 1)
                if e:
                    for s in range(3):
                        act.wait_ge(x_stored[s], 16 * x_stores[s])

            norm(0)

            _, p0, s0, o0, _ = BASE["R"]
            with act.Fori(0, RH) as h:
                pj, sj = h * R_PROJ + (CR + p0), h * R_SCORE + (CR + s0)

                def hi(j, dst, scale=1.0):
                    act.wait_ge(proj_done, pj + (j + 1))
                    act.activation(dst, proj_bank[j % 2][:, :], ACT.Copy, scale=scale).then_inc(proj_hi, 1)
                for j in range(8):
                    dst, u, th = (r_qT, r_kT)[j // 4], j // 2 % 2, j % 2
                    hi(j, dst[0][:, u, part(th, HALF)], 1.0 if j < 4 else DK ** -0.5)
                for b in range(TB):
                    hi(8 + b, r_v[0][:, b, :])
                    if b == 1:
                        act.wait_ge(mask_ready, h * 4 + 4)
                        act.activation(mask[:, :], mask[:, :], ACT.Exp).then_inc(mask_exp, 1)
                for th in range(2):
                    for b in range(TB):
                        j = 8 * th + b
                        act.wait_ge(score_free, sj + (9 * th + b + 1))
                        if b >= 2:
                            act.wait_ge(pv_done, h * 14 + (CR + 7 * th + b - 1))
                        else:
                            act.wait_ge(out_done, h * 8 + (CR + 4 * th))
                        act.activation(r_aT[0][:, b % 2, :], r_am[:, b % 2, :], ACT.Copy).then_inc(aT_hi_ready, 1)
                    act.wait_ge(aT_ready, h * 16 + (CR + 8 * th + 8))
                    for dt, dst in enumerate((r_am[:, 0, :], r_am[:, 1, :], r_e[:, :], r_sd[:, :])):
                        act.wait_ge(out_done, h * 8 + (CR + 4 * th + dt + 1))
                        act.activation(dst, out_bank[dt][:, :], ACT.Square).then_inc(sq_out, 1)
                    for dt in range(4):
                        act.wait_ge(mix_stored[dt], h * 32 + (16 + 16 * th))
                        act.activation(r_os[:, dt, :], out_bank[dt][:, :], ACT.Copy).then_inc(out_free, 1)
                    act.wait_ge(score_done, sj + (9 * th + 9))
                    act.activation(r_sd[:, :], score_bank[(9 * th + 8) % 2][:, :], ACT.Sqrt, bias=eps_t[:, :],
                                   scale=1.0 / DV).then_inc(score_free, 1)
                    for dt in range(4):
                        j = 16 + 4 * th + dt
                        act.wait_ge(proj_done, pj + (j + 1))
                        act.activation(r_e[:, :], proj_bank[j % 2][:, :], ACT.Sigmoid).then_inc(e_ready, 1)
                        act.wait_ge(gated, h * 8 + (4 * th + dt + 1))
                        act.dma_start(mix[bass.ds(h * DV + dt * P, P), part(th, HALF)], r_os[:, dt, :]) \
                           .then_inc(mix_stored[dt], 16)

            def mlp(phase):
                _, p0, _, o0, f0 = BASE[phase]

                def group(g, par):
                    for j in range(4):
                        th, u = j // 2, j % 2
                        act.wait_ge(sq_ready, g * M_PROJ + (f0 + CR + j - 1))
                        act.wait_ge(proj_done, g * M_PROJ + (CR + p0 + j + 1))
                        act.activation(relu[:, j % 2, :], proj_bank[j % 2][:, :], ACT.Relu).then_inc(proj_free, 1)
                        if j == 0:
                            act.wait_ge(out_done, g * G_OUT + (CR + o0 - G_OUT))
                        act.wait_ge(proj_free, g * M_PROJ + (CR + p0 + j + 1))
                        act.activation(aT[0][:, par, u, part(th, HALF)], relu[:, j % 2, :], ACT.Square).then_inc(ff_hi, 1)
                group(0, 0)
                with act.Fori(0, N_M // 2 - 1) as i:
                    group(i * 2 + 1, 1)
                    group(i * 2 + 2, 0)
                group(N_M - 1, 1)

            norm(1)
            mlp("M0")
            norm(2)

            _, p0, s0, _, _ = BASE["A"]
            with act.Fori(0, 2) as gp:
                pj, cj = gp * A_PROJ + (CR + p0), gp * A_CORE
                for j in range(18):
                    act.wait_ge(proj_done, pj + (j + 1))
                    src = proj_bank[j % 2]
                    if j < 8:
                        act.activation(a_qT[0][:, j // 2, part(j % 2, HALF)], src[:, :], ACT.Copy, scale=HD ** -0.5) \
                           .then_inc(proj_hi, 1)
                    elif j < 10:
                        act.activation(a_kT[0][:, part(j % 2, HALF)], src[:, :], ACT.Copy).then_inc(proj_hi, 1)
                    else:
                        act.activation(a_v[0][:, j - 10, :], src[:, 0:P], ACT.Copy).then_inc(proj_hi, 1)
                done = 0
                ends = [0]
                for st in range(A_CORE + 4):
                    c = st - 1
                    if 0 <= c < A_CORE:
                        nk = len(A_BLOCKS[c // 2]) * P
                        act.wait_ge(max_ready, cj + (c + 1))
                        for head in range(4):
                            s = a_s[:, c % 4, head, 0:nk]
                            act.activation(s, s, ACT.Exp, bias=nmax[:, c % 2, head:head + 1],
                                           accum_out=row_sum[:, c % 2, head:head + 1])
                        act.activation(sink_exp[:, c % 2, :], sink_gap[:, c % 2, :], ACT.Exp).then_inc(exp_ready, 1)
                    c = st - 3
                    if 0 <= c < A_CORE:
                        for i in range(len(A_BLOCKS[c // 2])):
                            j = 18 + done
                            act.wait_ge(attn_done, gp * A_PT + (CR + done - 3))
                            act.wait_ge(proj_done, pj + (j + 1))
                            act.activation(a_pT[0][:, done % 4, :], proj_bank[j % 2][:, :], ACT.Copy).then_inc(proj_hi, 1)
                            done += 1
                        ends.append(done)
                    c = st - 4
                    if 0 <= c < A_CORE:
                        b, two = c // 2, c % 2
                        rows = slice(HD * two, HD * two + HD)
                        act.wait_ge(attn_done, gp * A_PT + (CR + ends[c + 1]))
                        act.wait_ge(attn_out[c % 2], gp * (8 * A_CORE) + 16 * (1 + c // 2))
                        act.activation(a_out[rows, c % 2, :], out_bank[c % 4][rows, :], ACT.Copy).then_inc(attn_free, 1)
                        act.wait_ge(attn_free, cj + (CR + c + 1))
                        act.dma_start(mix[bass.ds(gp * (8 * HD) + 4 * HD * two, 4 * HD), part(b)]
                                      .rearrange("(j d) t -> d j t", d=HD),
                                      a_out[rows, c % 2, :].rearrange("d (j t) -> d j t", j=4)) \
                           .then_inc(attn_out[c % 2], 16)
            for s in attn_out:
                act.wait_ge(s, ATTN_STORES)
            norm(3)
            mlp("M1")
            norm(4)

        @block.vector
        def _(dve):
            step = Steps(dve, dve_step)
            gains = [0]

            def minus(dst, src, hi, scale=None):
                if scale is None:
                    return dve.tensor_tensor(dst, src, hi.bitcast(f32), ALU.subtract)
                return dve.scalar_tensor_tensor(out=dst, in0=src, scalar=scale, in1=hi.bitcast(f32), op0=ALU.mult,
                                                op1=ALU.subtract)

            def add_tile(first_job, j, tb, first=False):
                dst, src = y[:, tb, part(j % 2, HALF)], out_bank[j % 4][:, :]
                dve.wait_ge(out_done, first_job + (j + 1))
                if first:
                    dve.tensor_copy(dst, src).then_inc(out_free, 1)
                else:
                    dve.tensor_tensor(dst, dst, src, ALU.add).then_inc(out_free, 1)

            def add_group(first_job, first=False):
                dve.wait_ge(out_free, first_job)
                for j in range(G_OUT):
                    add_tile(first_job, j, j // 2, first)

            def norm(e):
                phase = f"E{e}"
                s0, o0 = BASE[phase][2], BASE[phase][3]
                tail = CR + o0 - TAIL
                gains[0] += 16 * ((post[e] is not None) + (pre[e] is not None))
                if e:
                    dve.wait_ge(out_free, tail)
                    for j in range(8):
                        add_tile(tail, j, 4 + j // 2)
                    dve.wait_ge(out_free, tail + 8)
                for st in range(TB + 3):
                    tb = st
                    if e and tb < TB:
                        add_tile(tail, 8 + 2 * tb, tb)
                        add_tile(tail, 9 + 2 * tb, tb)
                    tb = st - 3
                    if e < 4 and 0 <= tb < TB:
                        for j in range(2):
                            dve.wait_ge(hT_hi_ready, e * 2 * TB + 2 * tb + j + 1)
                            four = slice(4 * j, 4 * j + 4)
                            minus(hT[1][:, four, part(tb)], score_bank[j][:, :].rearrange("p (k t) -> p k t", k=4),
                                  hT[0][:, four, part(tb)]).then_inc(score_free, 1)
                    tb = st
                    if e and tb < TB:
                        dve.wait_ge(std_y, (e - 1) * TB + tb + 1)
                        step(dve.reciprocal(stats[:, 4, tb:tb + 1], stats[:, 1, tb:tb + 1]))
                        if tb == 0:
                            dve.wait_ge(gains_loaded, gains[0])
                        dve.scalar_tensor_tensor(out=y[:, tb, :], in0=y[:, tb, :], scalar=stats[:, 4, tb:tb + 1],
                                                 in1=gain_post[:, :], op0=ALU.mult, op1=ALU.mult).then_inc(z_ready, 1)
                    tb = st - 1
                    if e < 4 and 0 <= tb < TB:
                        dve.wait_ge(std_x, e * TB + tb + 1)
                        step(dve.reciprocal(stats[:, 5, tb:tb + 1], stats[:, 3, tb:tb + 1]))
                        if e == 0 and tb == 0:
                            dve.wait_ge(gains_loaded, gains[0])
                        dve.scalar_tensor_tensor(out=xn[:, tb % 2, :], in0=xt[:, tb % 3, :],
                                                 scalar=stats[:, 5, tb:tb + 1], in1=gain_pre[:, :], op0=ALU.mult,
                                                 op1=ALU.mult).then_inc(xn_ready, 1)

            dve.wait_ge(consts, 6 + AH)
            dve.tensor_copy(dist16[:, :], dist_i[:, :])
            dve.wait_ge(params, 48)
            step(dve.tensor_scalar(decay[:, 1, :], decay[:, 1, :], -1.0, None, ALU.mult))
            norm(0)

            _, p0, s0, o0, _ = BASE["R"]
            PIECE = MASK // 4
            with dve.Fori(0, RH) as h:
                step.enter(h, 1 + 4 + 2 * (1 + 1 + 4))
                pj, sj = h * R_PROJ + (CR + p0), h * R_SCORE + (CR + s0)
                step(dve.tensor_copy(decay_now[:, :].unsqueeze(2), decay[:, :, bass.ds(h, 1)]))
                for j in range(8):
                    pair, u, th = (r_qT, r_kT)[j // 4], j // 2 % 2, j % 2
                    dve.wait_ge(proj_hi, h * 16 + (j + 1))
                    dst = cut(pair, u, part(th, HALF))
                    minus(dst[1], proj_bank[j % 2][:, :], dst[0], None if j < 4 else DK ** -0.5).then_inc(proj_free, 1)
                    if j >= 4:
                        m = slice((j - 4) * PIECE, (j - 3) * PIECE)
                        tmp = r_am[:, 0, 0:PIECE]
                        dve.tensor_scalar(mask[:, m], dist16[:, m], 0.0, decay_now[:, 0:1], ALU.max, ALU.mult)
                        step(dve.tensor_scalar(tmp, dist16[:, m], 0.0, decay_now[:, 1:2], ALU.min, ALU.mult))
                        ins = dve.tensor_tensor(mask[:, m], mask[:, m], tmp, ALU.add)
                        ins.then_inc(mask_ready, 1)
                        dve.wait_ge(mask_ready, h * 4 + (j - 3))
                for b in range(TB):
                    dve.wait_ge(proj_hi, h * 16 + (9 + b))
                    minus(r_v[1][:, b, :], proj_bank[b % 2][:, :], r_v[0][:, b, :]).then_inc(proj_free, 1)
                dve.wait_ge(mask_exp, h + 1)
                for th in range(2):
                    for b in range(TB):
                        j = 8 * th + b
                        dve.wait_ge(aT_hi_ready, h * 16 + (CR + j - 1))
                        dve.wait_ge(score_done, sj + (9 * th + b + 1))
                        at = th * HALF + (TB - 1 - b) * P
                        dve.tensor_tensor(r_am[:, b % 2, :], score_bank[(9 * th + b) % 2][:, :],
                                          mask[:, at:at + HALF], ALU.mult).then_inc(score_free, 1)
                        dve.wait_ge(aT_hi_ready, h * 16 + (CR + j + 1))
                        minus(r_aT[1][:, b % 2, :], r_am[:, b % 2, :], r_aT[0][:, b % 2, :]).then_inc(aT_ready, 1)
                    dve.wait_ge(sq_out, h * 8 + (4 * th + 4))
                    dve.tensor_tensor(r_am[:, 0, :], r_am[:, 0, :], r_am[:, 1, :], ALU.add)
                    step(dve.tensor_tensor(r_e[:, :], r_e[:, :], r_sd[:, :], ALU.add))
                    dve.tensor_tensor(r_am[:, 0, :], r_am[:, 0, :], r_e[:, :], ALU.add).then_inc(sq_sum, 1)
                    dve.wait_ge(score_free, sj + (9 * th + 9))
                    step(dve.reciprocal(r_sd[:, :], r_sd[:, :]))
                    for dt in range(4):
                        j = 16 + 4 * th + dt
                        step(dve.tensor_tensor(r_os[:, dt, :], r_os[:, dt, :], r_sd[:, :], ALU.mult))
                        dve.wait_ge(e_ready, h * 8 + (4 * th + dt + 1))
                        dve.tensor_tensor(r_os[:, dt, :], r_os[:, dt, :], proj_bank[j % 2][:, :], ALU.mult) \
                           .then_inc(proj_free, 1)
                        dve.wait_ge(proj_free, pj + (j + 1))
                        dve.tensor_tensor(r_os[:, dt, :], r_os[:, dt, :], r_e[:, :], ALU.mult).then_inc(gated, 1)
            step.leave(RH)

            def outputs(phase, groups):
                o0 = BASE[phase][3]
                add_group(CR + o0, first=True)
                with dve.Fori(1, groups - 2) as g:
                    add_group(g * G_OUT + (CR + o0))

            def mlp(phase):
                _, p0, _, o0, f0 = BASE[phase]

                def hidden(g, par):
                    for j in range(4):
                        th, u = j // 2, j % 2
                        dve.wait_ge(proj_free, g * M_PROJ + (CR + p0 + j + 1))
                        r = relu[:, j % 2, :]
                        dve.tensor_tensor(relu_sq[:, j % 2, :], r, r, ALU.mult).then_inc(sq_ready, 1)
                        dve.wait_ge(sq_ready, g * M_PROJ + (f0 + CR + j + 1))
                        dve.wait_ge(ff_hi, g * M_PROJ + (f0 + j + 1))
                        dst = cut(aT, par, u, part(th, HALF))
                        minus(dst[1], relu_sq[:, j % 2, :], dst[0]).then_inc(ff_ready, 1)
                hidden(0, 0)
                hidden(1, 1)
                add_group(CR + o0, first=True)
                with dve.Fori(0, N_M // 2 - 2) as i:
                    for par in range(2):
                        g = i * 2 + (1 + par)
                        hidden(g + 1, par)
                        add_group(g * G_OUT + (CR + o0))
                g = N_M - 3
                hidden(g + 1, 0)
                add_group(g * G_OUT + (CR + o0))
                hidden(g + 2, 1)

            outputs("O0", N_O0)
            norm(1)
            mlp("M0")
            norm(2)

            _, p0, s0, _, _ = BASE["A"]
            h0 = 16 * RH
            step(dve.tensor_copy(a_dist[:, :], a_iota[:, :]))
            step(dve.tensor_scalar(a_far[:, :], a_dist[:, :], -1.0, None, ALU.mult))
            step(dve.tensor_tensor(a_dist[:, :], a_dist[:, :], a_far[:, :], ALU.max))
            step(dve.tensor_scalar(a_far[:, :], a_dist[:, :], float(P), BIG, ALU.is_gt, ALU.mult))
            step(dve.tensor_tensor(a_dist[:, :], a_dist[:, :], a_far[:, :], ALU.add))
            with dve.Fori(0, 2) as gp:
                step.enter(gp, 1 + 4 * A_CORE)
                pj, sj, cj = gp * A_PROJ + (CR + p0), gp * A_SCORE + (CR + s0), gp * A_CORE
                dve.tensor_copy(slope_now[:, :], slope[:, bass.ds(gp * 8, 8)])
                step(dve.tensor_copy(sink_now[:, :], sink[:, bass.ds(gp * 8, 8)]))
                for j in range(18):
                    dve.wait_ge(proj_hi, gp * A_PROJ + (h0 + j + 1))
                    src = proj_bank[j % 2]
                    if j < 8:
                        dst = cut(a_qT, j // 2, part(j % 2, HALF))
                        minus(dst[1], src[:, :], dst[0], HD ** -0.5).then_inc(proj_free, 1)
                    elif j < 10:
                        dst = cut(a_kT, part(j % 2, HALF))
                        minus(dst[1], src[:, :], dst[0]).then_inc(proj_free, 1)
                    else:
                        dst = cut(a_v, j - 10, slice(None))
                        minus(dst[1], src[:, 0:P], dst[0]).then_inc(proj_free, 1)
                done = 0
                for st in range(A_CORE + 3):
                    c = st - 3
                    if c >= 0:
                        for i in range(len(A_BLOCKS[c // 2])):
                            dve.wait_ge(proj_hi, gp * A_PROJ + (h0 + 18 + done + 1))
                            dst = cut(a_pT, done % 4)
                            minus(dst[1], proj_bank[done % 2][:, :], dst[0]).then_inc(proj_free, 1)
                            done += 1
                    if st < A_CORE:
                        b, two = st // 2, st % 2
                        blocks = A_BLOCKS[b]
                        nk, left = len(blocks) * P, (blocks[0] - b + 1) * P
                        heads = slice(4 * two, 4 * two + 4)
                        for head in range(4):
                            dve.wait_ge(score_done, sj + (4 * st + head + 1))
                            dve.scalar_tensor_tensor(out=a_s[:, st % 4, head, 0:nk], in0=a_dist[:, left:left + nk],
                                                     scalar=slope_now[:, 4 * two + head:4 * two + head + 1],
                                                     in1=score_bank[head % 2][:, 0:nk], op0=ALU.mult, op1=ALU.add) \
                               .then_inc(score_free, 1)
                    c = st - 1
                    if 0 <= c < A_CORE:
                        k = c % 2
                        dve.wait_ge(exp_ready, cj + (c + 1))
                        step(dve.tensor_tensor(row_sum[:, k, :], row_sum[:, k, :], sink_exp[:, k, :], ALU.add))
                        dve.reciprocal(row_inv[:, k, :], row_sum[:, k, :]).then_inc(inv_ready, 1)
                    if st < A_CORE:
                        k = st % 2
                        dve.wait_ge(score_free, sj + (4 * st + 4))
                        step(dve.reduce_max(smax[:, k, :], a_s[:, st % 4, :, 0:nk], AX.X))
                        step(dve.tensor_tensor(smax[:, k, :], smax[:, k, :], sink_now[:, heads], ALU.max))
                        step(dve.tensor_scalar(nmax[:, k, :], smax[:, k, :], -1.0, None, ALU.mult))
                        dve.tensor_tensor(sink_gap[:, k, :], sink_now[:, heads], nmax[:, k, :], ALU.add) \
                           .then_inc(max_ready, 1)
            step.leave(2)

            outputs("O1", N_O1)
            norm(3)
            mlp("M1")
            norm(4)


_INS = ["x", "w_in_ret", "w_out_ret", "log_decay_fwd", "log_decay_bwd", "w_in_attn", "w_out_attn", "sink_logits",
        "g_pre_mix", "g_post_mix", "g_pre_mlp", "g_post_mlp", "w_up", "w_down"]


def kernel(**inputs):
    import numpy as np
    import concourse.bacc as bacc
    from concourse.bass_utils import run_bass_kernel_spmd

    nc = bacc.Bacc("TRN2", target_bir_lowering=False, num_devices=1)
    arrays, args = {}, []
    for name in _INS:
        a = np.ascontiguousarray(inputs[name])
        arrays[f"in_{name}"] = a
        args.append(nc.dram_tensor(f"in_{name}", a.shape, mybir.dt.from_np(a.dtype), kind="ExternalInput").ap())
    args.append(nc.dram_tensor("result", (1, T, D), mybir.dt.float32, kind="ExternalOutput").ap())
    build(nc, *args)
    r = run_bass_kernel_spmd(nc, [arrays], core_ids=[0])
    return r.results[0]["result"]
```

```python
import concourse.bass as bass
from concourse import mybir

P = 128
D = 1024
T = 1024
KT = D // P
TB = T // P
HALF = 512
RH, DK, DV = 4, 256, 512
NQ, NV = RH * DK, RH * DV
AH, AG, HD = 16, 4, 64
FF = 4 * D
EPS = 1e-6
BIG = 1e30

RAW = 2
WS = 4
UNIT = 1024
CR = 4

R_UNITS, R_PROJ, R_SCORE, R_OUT = 16, 24, 18, 8
G_UNITS, G_OUT = 4, 16
LONE = 3
TAIL = G_OUT + 2 * LONE
M_PROJ = 4
A_UNITS, A_CORE, A_SCORE = 6, 16, 64
A_BLOCKS = [[kb for kb in (b - 1, b, b + 1) if 0 <= kb < TB] for b in range(TB)]
A_PT = 2 * sum(len(x) for x in A_BLOCKS)
A_PROJ = 18 + A_PT
A_PT_SLOTS = 5
N_O0, N_O1, N_M = NV // (2 * P), D // (2 * P), FF // (2 * P)


def bases():
    unit = proj = score = out = ff = 0
    b = {}

    def at(name):
        b[name] = (unit, proj, score, out, ff)
    at("E0"); score += 16
    at("R"); unit += RH * R_UNITS; proj += RH * R_PROJ; score += RH * R_SCORE; out += RH * R_OUT
    at("O0"); unit += N_O0 * G_UNITS; out += (N_O0 - 2) * G_OUT + TAIL
    at("E1"); score += 16
    at("M0"); unit += N_M * G_UNITS; proj += N_M * M_PROJ; out += (N_M - 2) * G_OUT + TAIL; ff += N_M * M_PROJ
    at("E2"); score += 16
    at("A"); unit += 2 * A_UNITS; proj += 2 * A_PROJ; score += 2 * A_SCORE
    at("O1"); unit += N_O1 * G_UNITS; out += (N_O1 - 2) * G_OUT + TAIL
    at("E3"); score += 16
    at("M1"); unit += N_M * G_UNITS; proj += N_M * M_PROJ; out += (N_M - 2) * G_OUT + TAIL; ff += N_M * M_PROJ
    at("E4")
    return b


BASE = bases()


def loads_before(phase):
    return 16 * BASE[phase][0] // RAW + (2 * 2 * 16 if phase in ("O1", "M1") else 0)


class Steps:

    def __init__(self, eng, sem):
        self.eng, self.sem, self.n, self.base = eng, sem, 0, 0

    def __call__(self, ins):
        ins.then_inc(self.sem, 1)
        self.n += 1
        self.eng.wait_ge(self.sem, self.base + self.n)

    def enter(self, i, stride):
        self.start, self.stride, self.base = self.n, stride, i * stride

    def leave(self, rounds):
        assert self.n - self.start == self.stride, (self.n - self.start, self.stride)
        self.n, self.base = self.start + rounds * self.stride, 0


def build(nc, x, w_in_ret, w_out_ret, log_decay_fwd, log_decay_bwd, w_in_attn, w_out_attn, sink_logits,
          g_pre_mix, g_post_mix, g_pre_mlp, g_post_mlp, w_up, w_down, out):
    f32, f32r, f16, i32 = mybir.dt.float32, mybir.dt.float32r, mybir.dt.float16, mybir.dt.int32
    ACT, ALU, AX = mybir.ActivationFunctionType, mybir.AluOpType, mybir.AxisListType

    at = [(nc.sbuf_base + 63) // 64 * 64]

    def sb(name, shape, dt, offset=None):
        size = 4
        for s in shape[1:]:
            size *= s
        size = (size // 2 if dt == f16 else size) + 31 & -32
        if offset is None:
            offset, at[0] = at[0], at[0] + size
        assert offset + size <= nc.sbuf_usable_end, (name, offset + size, nc.sbuf_usable_end)
        return nc.alloc_sbuf_tensor_at(name, shape, dt, offset=offset)

    hT = [sb("hT_hi", [P, KT, T], f32r), sb("hT_lo", [P, KT, T], f32r)]
    w_raw = sb("w_raw", [P, RAW, UNIT], f32)
    w_split = [sb("w_hi", [P, WS, UNIT], f32r), sb("w_lo", [P, WS, UNIT], f32r)]
    ident = sb("ident", [P, P], f32)
    ones = sb("ones", [P, P], f32)
    one = ones[:, 0:1]
    stats = sb("stats", [P, 6, TB], f32)
    eps_t = sb("eps_t", [P, 1], f32)
    decay = sb("decay", [P, 2, RH], f32)
    decay_now = sb("decay_now", [P, 2], f32)
    slope = sb("slope", [P, AH], f32)
    slope_now = sb("slope_now", [P, 8], f32)
    sink = sb("sink", [P, AH], f32)
    sink_now = sb("sink_now", [P, 8], f32)
    nmax = sb("nmax", [P, 2, 4], f32)
    row_sum = sb("row_sum", [P, 2, 4], f32)
    row_inv = sb("row_inv", [P, 2, 4], f32)
    a_iota = sb("a_iota", [P, 3 * P], i32)
    arena = (at[0] + 63) // 64 * 64

    at[0] = arena
    r_qT = [sb("r_qT_hi", [P, 2, T], f32r), sb("r_qT_lo", [P, 2, T], f32r)]
    r_kT = [sb("r_kT_hi", [P, 2, T], f32r), sb("r_kT_lo", [P, 2, T], f32r)]
    r_v = [sb("r_v_hi", [P, TB, DV], f32r), sb("r_v_lo", [P, TB, DV], f32r)]
    MASK = 2 * T - P
    dist16 = sb("dist16", [P, MASK], f16)
    r_aT = [sb("r_aT_hi", [P, 2, HALF], f32r), sb("r_aT_lo", [P, 2, HALF], f32r)]
    mask = sb("mask", [P, MASK], f32)
    r_am = sb("r_am", [P, 2, HALF], f32)
    r_os = sb("r_os", [P, 4, HALF], f32)
    r_e = sb("r_e", [P, HALF], f32)
    r_sd = sb("r_sd", [P, HALF], f32)

    dist_i = sb("dist_i", [P, MASK], i32, offset=arena + 4 * 8 * T)

    at[0] = arena
    aT = [sb("aT_hi", [P, 2, 2, T], f32r), sb("aT_lo", [P, 2, 2, T], f32r)]
    y = sb("y", [P, TB, D], f32)
    relu = sb("relu", [P, 2, HALF], f32)
    relu_sq = sb("relu_sq", [P, 2, HALF], f32)
    squares = relu_sq[:, :, :].rearrange("p a t -> p (a t)")
    xt = sb("xt", [P, 3, D], f32)
    xn = sb("xn", [P, 2, D], f32)
    gain_post = sb("gain_post", [P, D], f32)
    gain_pre = sb("gain_pre", [P, D], f32)

    at[0] = arena
    a_qT = [sb("a_qT_hi", [P, 4, T], f32r), sb("a_qT_lo", [P, 4, T], f32r)]
    a_kT = [sb("a_kT_hi", [P, T], f32r), sb("a_kT_lo", [P, T], f32r)]
    a_v = [sb("a_v_hi", [P, TB, P], f32r), sb("a_v_lo", [P, TB, P], f32r)]
    a_pT = [sb("a_pT_hi", [P, A_PT_SLOTS, HALF], f32r), sb("a_pT_lo", [P, A_PT_SLOTS, HALF], f32r)]
    a_s = sb("a_s", [P, 4, 4, 1 + 3 * P], f32)
    a_out = sb("a_out", [P, 2, HALF], f32)
    a_dist = sb("a_dist", [P, 3 * P], f32)
    a_far = sb("a_far", [P, 3 * P], f32)

    banks = [nc.alloc_psum_tensor(f"bank{i}", [P, HALF], f32) for i in range(8)]
    score_bank, proj_bank, out_bank = banks[0:2], banks[2:4], banks[4:8]
    attn_score_bank = banks[0:2] + banks[6:8]

    mix = nc.dram_tensor("mix", (NV, T), f32).ap()
    x_mid = [nc.dram_tensor(f"x_mid{i}", (T, D), f32).ap() for i in range(3)]
    x_in = [x[0], x[0], x_mid[0], x_mid[1], x_mid[2]]
    x_out = [None, x_mid[0], x_mid[1], x_mid[2], out[0]]
    post = [None, g_post_mix[0], g_post_mlp[0], g_post_mix[1], g_post_mlp[1]]
    pre = [g_pre_mix[0], g_pre_mlp[0], g_pre_mix[1], g_pre_mlp[1], None]

    sem = nc.alloc_semaphore
    raw_loaded = [sem(f"raw_loaded{i}") for i in range(RAW)]
    unit_hi = sem("unit_hi")
    unit_hi_scalar = sem("unit_hi_scalar")
    unit_split = sem("unit_split")
    proj_done, proj_free = sem("proj_done"), sem("proj_free")
    score_done, score_free = sem("score_done"), sem("score_free")
    out_done, out_free = sem("out_done"), sem("out_free")
    proj_hi = sem("proj_hi")
    consts = sem("consts")
    params = sem("params")
    act_step, dve_step = sem("act_step"), sem("dve_step")
    gains_loaded = sem("gains_loaded")
    x_loaded = [sem(f"x_loaded{i}") for i in range(3)]
    x_stored = [sem(f"x_stored{i}") for i in range(3)]
    std_y, std_x = sem("std_y"), sem("std_x")
    z_ready = sem("z_ready")
    x_new = sem("x_new")
    xn_ready = sem("xn_ready")
    hT_hi_ready = sem("hT_hi_ready")
    sq_ready = sem("sq_ready")
    ff_hi = sem("ff_hi")
    ff_ready = sem("ff_ready")
    mask_ready = sem("mask_ready")
    mask_exp = sem("mask_exp")
    aT_hi_ready = sem("aT_hi_ready")
    aT_ready = sem("aT_ready")
    pv_done = sem("pv_done")
    sq_out = sem("sq_out")
    sq_sum = sem("sq_sum")
    e_ready = sem("e_ready")
    gated = sem("gated")
    mix_stored = [sem(f"mix_stored{i}") for i in range(4)]
    max_ready = sem("max_ready")
    exp_ready = sem("exp_ready")
    inv_ready = sem("inv_ready")
    p_ready = sem("p_ready")
    attn_done, attn_free = sem("attn_done"), sem("attn_free")
    attn_out = [sem(f"attn_out{i}") for i in range(2)]
    credited = [unit_split, proj_done, proj_free, score_done, score_free, out_done, out_free,
                aT_hi_ready, aT_ready, pv_done, attn_done, attn_free, p_ready, sq_ready]

    def part(k, n=P):
        return slice(k * n, (k + 1) * n)

    def cut(pair, *idx):
        return [t[(slice(None), *idx)] for t in pair]

    def wslot(s, cols):
        return cut(w_split, s, cols)

    def output_slot(phase, par, u):
        k = u % 2
        return cut(aT, par, k) if (u < 2) == (phase == "O0") else wslot(2 * par + k, slice(None))

    ATTN_STORES = 16 * (1 + A_CORE)

    block = nc.Block()
    with block:

        @block.sync
        def _(sp):
            for s in credited:
                sp.sem_inc(s, CR)
            for s in mix_stored + attn_out:
                sp.sem_inc(s, 16)

            def load(n, slot, dst, src):
                sp.wait_ge(unit_split, CR + n - RAW + 1)
                sp.dma_start(dst, src).then_inc(raw_loaded[slot], 16)

            def by_column(slot):
                return w_raw[:, slot, :].rearrange("p (k c) -> p k c", k=KT)

            w_r = w_in_ret[0].rearrange("(k p) c -> p k c", p=P)
            with sp.Fori(0, RH) as h:
                n = h * R_UNITS
                idx = 0
                for c0 in (0, NQ):
                    for u in range(2):
                        load(n + idx, idx % RAW, by_column(idx % RAW), w_r[:, :, bass.ds(h * DK + (c0 + u * P), P)])
                        idx += 1
                for u in range(4):
                    load(n + idx, idx % RAW, w_raw[:, idx % RAW, :].rearrange("p (k c) -> p k c", k=2),
                         w_r[:, 2 * u:2 * u + 2, bass.ds(h * DV + 2 * NQ, DV)])
                    idx += 1
                for th in range(2):
                    for u in range(4):
                        load(n + idx, idx % RAW, by_column(idx % RAW),
                             w_r[:, :, bass.ds(h * DV + (2 * NQ + NV + u * P), P)])
                        idx += 1

            def load_outputs(phase, groups, w, stored, each):
                n0 = BASE[phase][0]
                with sp.Fori(0, groups // 2) as i:
                    stores = sp.snap(i * each + (16 + each))
                    slot_free = sp.snap(i * (2 * G_UNITS) + (n0 + CR - RAW + 1))
                    for st in stored:
                        sp.wait_ge(st, stores)
                    sp.wait_ge(unit_split, slot_free)
                    for par in range(2):
                        n, row = i * (2 * G_UNITS) + (n0 + G_UNITS * par), i * (4 * P) + 2 * P * par
                        sources = (w, mix) if phase == "O1" else (mix, w)
                        for u in range(4):
                            load(n + u, u % RAW, w_raw[:, u % RAW, :], sources[u // 2][bass.ds(row + u % 2 * P, P), :])

            def load_mlp(phase, layer):
                n0 = BASE[phase][0]
                up = w_up[layer].rearrange("(k p) c -> p k c", p=P)
                down = w_down[layer]
                for u in range(2):
                    load(n0 + u, u, by_column(u), up[:, :, part(u)])
                with sp.Fori(0, N_M - 1) as g:
                    for u in range(2):
                        load(g * G_UNITS + (n0 + 2 + u), u, by_column(u), up[:, :, bass.ds(g * (2 * P) + (2 + u) * P, P)])
                    for u in range(2):
                        load(g * G_UNITS + (n0 + 4 + u), u, w_raw[:, u, :], down[bass.ds(g * (2 * P) + u * P, P), :])
                for u in range(2):
                    load(n0 + (N_M - 1) * G_UNITS + 2 + u, u, w_raw[:, u, :], down[part(2 * (N_M - 1) + u), :])

            load_outputs("O0", N_O0, w_out_ret[0], mix_stored, 16 * 2)
            load_mlp("M0", 0)

            wa = w_in_attn[0].rearrange("(k p) c -> p k c", p=P)
            n0 = BASE["A"][0]
            with sp.Fori(0, 2) as gp:
                n = gp * A_UNITS + n0
                for j in range(4):
                    s = j % RAW
                    sp.wait_ge(unit_split, n + (CR + j - RAW + 1))
                    for two in range(2):
                        dst = w_raw[:, s, :].rearrange("p (k two c) -> p k two c", k=KT, two=2)[:, :, two, :]
                        sp.dma_start(dst, wa[:, :, bass.ds(gp * (8 * HD) + (4 * two + j) * HD, HD)]) \
                          .then_inc(raw_loaded[s], 16)
                for u in range(2):
                    load(n + (4 + u), u, by_column(u), wa[:, :, bass.ds(gp * P + (AH * HD + u * AG * HD), P)])

            load_outputs("O1", N_O1, w_out_attn[0], attn_out, 16 * A_CORE // 2)
            load_mlp("M1", 1)

        @block.gpsimd
        def _(pool):
            pool.memset(ident[:, :], 0.0).then_inc(consts, 1)
            pool.wait_ge(consts, 1)
            pool.affine_select(out=ident[:, :], in_=ident[:, :], compare_op=ALU.not_equal, fill=1.0, base=0,
                               pattern=[[-1, P]], channel_multiplier=1).then_inc(consts, 1)
            pool.memset(ones[:, :], 1.0).then_inc(consts, 1)
            pool.memset(eps_t[:, :], EPS).then_inc(consts, 1)
            for i in range(AH):
                pool.memset(slope[:, i:i + 1], -2.0 ** (-8.0 * (i + 1) / AH)).then_inc(consts, 1)
            pool.iota(dist_i[:, :], pattern=[[1, MASK]], base=-(T - P), channel_multiplier=-1).then_inc(consts, 1)
            pool.iota(a_iota[:, :], pattern=[[1, 3 * P]], base=-P, channel_multiplier=-1).then_inc(consts, 1)
            pool.wait_ge(consts, 6 + AH)

            scalar_units = [0]

            def cut_unit(slot, loaded, dst, n):
                pool.wait_ge(raw_loaded[slot], loaded)
                raw = w_raw[:, slot, :]
                pool.tensor_tensor(dst[0], raw, one.broadcast_to([P, UNIT]), ALU.mult).then_inc(unit_hi, 1)
                pool.wait_ge(unit_hi, n + (1 - scalar_units[0]))
                pool.tensor_tensor(dst[1], raw, dst[0].bitcast(f32), ALU.subtract).then_inc(unit_split, 1)

            with pool.Fori(0, RH) as h:
                for i in range(R_UNITS):
                    free_at = {0: -3, 1: -2, 2: -1, 3: 0, 4: 2, 5: 4, 6: 6, 7: 8}.get(i, 16 if i < 12 else 17 + i - 12)
                    pool.wait_ge(proj_done, h * R_PROJ + (CR + free_at))
                    cut_unit(i % RAW, h * (16 * R_UNITS // RAW) + 16 * (i // RAW + 1), wslot(i % WS, slice(None)),
                             h * R_UNITS + i)

            def cut_lo(slot, dst, m):
                pool.wait_ge(unit_hi_scalar, m + 1)
                pool.tensor_tensor(dst[1], w_raw[:, slot, :], dst[0].bitcast(f32), ALU.subtract).then_inc(unit_split, 1)

            def cut_first_output(phase, u, wait):
                pool.wait_ge(*wait)
                cut_unit(u % RAW, loads_before(phase) + 16 * (u // RAW + 1), output_slot(phase, 0, u),
                         BASE[phase][0] + u)

            def cut_outputs(phase, groups):
                m0 = scalar_units[0]
                for u in range(4):
                    cut_lo(u % RAW, output_slot(phase, 1, u), m0 + u)
                with pool.Fori(1, groups // 2) as i:
                    for par in range(2):
                        for u in range(4):
                            cut_lo(u % RAW, output_slot(phase, par, u), i * (2 * G_UNITS) + (m0 + G_UNITS * (par - 1) + u))
                scalar_units[0] += (groups - 1) * G_UNITS

            def add_residual(e, between):
                for tb in range(TB):
                    s = tb % 3
                    pool.wait_ge(x_loaded[s], 16 * (e * (3, 3, 2)[s] + tb // 3 + 1))
                    pool.wait_ge(z_ready, (e - 1) * TB + tb + 1)
                    pool.tensor_tensor(xt[:, s, :], xt[:, s, :], y[:, tb, :], ALU.add).then_inc(x_new, 1)
                    if tb in between:
                        between[tb]()

            def cut_mlp(phase, e):
                n0, p0, _, o0, _ = BASE[phase]
                loaded0 = loads_before(phase)

                def first(u):
                    pool.wait_ge(out_done, CR + o0 - 2 * LONE)
                    cut_unit(u, loaded0 + 16, wslot(u, slice(None)), n0 + u)
                add_residual(e, {3: lambda: first(0), 5: lambda: first(1)})
                pool.wait_ge(out_done, CR + o0)
                for u in range(2):
                    cut_unit(u, loaded0 + 32, wslot(2 + u, slice(None)), n0 + 2 + u)
                pool.wait_ge(proj_done, CR + p0 + M_PROJ)
                for u in range(2):
                    cut_unit(u, loaded0 + 48, wslot(u, slice(None)), n0 + 4 + u)
                with pool.Fori(1, N_M - 1) as g:
                    for u in range(2):
                        pool.wait_ge(proj_done, g * M_PROJ + (CR + p0 + 3 + u))
                        cut_unit(u, g * 32 + (loaded0 + 32), wslot(2 + u, slice(None)), g * G_UNITS + (n0 + 2 + u))
                    for u in range(2):
                        pool.wait_ge(out_done, g * G_OUT + (CR + o0))
                        cut_unit(u, g * 32 + (loaded0 + 48), wslot(u, slice(None)), g * G_UNITS + (n0 + 4 + u))
                g = N_M - 1
                for u in range(2):
                    pool.wait_ge(proj_done, CR + p0 + g * M_PROJ + 3 + u)
                    cut_unit(u, loaded0 + 32 + 32 * g, wslot(2 + u, slice(None)), n0 + 2 + g * G_UNITS + u)

            p_end = CR + RH * R_PROJ
            scores_read = (score_done, CR + BASE["R"][2] + RH * R_SCORE - 1)
            for u, wait in enumerate([scores_read, scores_read, (proj_done, p_end - 3), (proj_done, p_end - 2)]):
                cut_first_output("O0", u, wait)
            cut_outputs("O0", N_O0)
            cut_mlp("M0", 1)

            n0, p0, s0, o0, _ = BASE["A"]
            loaded0 = loads_before("A")

            def cut_q(gp, j):
                if gp:
                    pool.wait_ge(proj_done, CR + p0 + 18)
                else:
                    pool.wait_ge(out_done, CR + o0 - 2 * LONE * (j < 2))
                cut_unit(j % RAW, loaded0 + 80 * gp + 32 * (j // RAW + 1), wslot(j, slice(None)), n0 + gp * A_UNITS + j)
            add_residual(2, {3: lambda: cut_q(0, 0), 5: lambda: cut_q(0, 1)})
            for gp in range(2):
                if gp == 0:
                    cut_q(0, 2)
                    cut_q(0, 3)
                for u in range(2):
                    pool.wait_ge(proj_done, CR + p0 + gp * A_PROJ + 2 * (u + 1))
                    cut_unit(u, loaded0 + 80 * gp + 80, wslot(u, slice(None)), n0 + gp * A_UNITS + 4 + u)
                for c in range(A_CORE):
                    nk = len(A_BLOCKS[c // 2]) * P
                    pool.wait_ge(inv_ready, gp * A_CORE + c + 1)
                    s = a_s[:, c % 4, :, 1:1 + nk]
                    pool.tensor_tensor(s, s, row_inv[:, c % 2, :].unsqueeze(2).broadcast_to([P, 4, nk]), ALU.mult) \
                        .then_inc(p_ready, 1)
                    if gp == 0 and c in (2, 5, 8, 11):
                        cut_q(1, (c - 2) // 3)
                    if gp == 1 and c in (8, 11):
                        cut_first_output("O1", (c - 8) // 3, (proj_done, CR + p0 + A_PROJ + 18))
            for u in (2, 3):
                cut_first_output("O1", u, (score_done, CR + s0 + 2 * A_SCORE))
            cut_outputs("O1", N_O1)
            cut_mlp("M1", 3)
            add_residual(4, {})

        @block.tensor
        def _(pe):
            def mm3(dst, stat, mov, first, last):
                pe.matmul(dst, stat[0], mov[0], start=first, stop=False)
                pe.matmul(dst, stat[0], mov[1], start=False, stop=False)
                return pe.matmul(dst, stat[1], mov[0], start=False, stop=last)

            def unit_ready(n):
                pe.wait_ge(unit_split, n + (CR + 1))

            def transpose_norm(phase, tb):
                s0 = BASE[phase][2]
                pe.wait_ge(xn_ready, int(phase[1]) * TB + tb + 1)
                for j in range(2):
                    pe.wait_ge(score_free, CR + s0 + 2 * tb + j - 1)
                    for k in range(4):
                        mm = pe.transpose(score_bank[j][:, part(k)], xn[:, tb % 2, part(4 * j + k)], ident[:, :])
                    mm.then_inc(score_done, 1)

            def hT_ready(phase, halves):
                pe.wait_ge(score_free, CR + BASE[phase][2] + 8 * halves)

            def project(slot, th, bank, free):
                pe.wait_ge(proj_free, free)
                for k in range(KT):
                    mm = mm3(proj_bank[bank][:, :], wslot(slot, part(k)), cut(hT, k, part(th, HALF)), k == 0, k == KT - 1)
                mm.then_inc(proj_done, 1)

            pe.wait_ge(consts, 4)
            for tb in range(TB):
                transpose_norm("E0", tb)
            hT_ready("E0", 2)

            _, p0, s0, o0, _ = BASE["R"]
            with pe.Fori(0, RH) as h:
                n, pj, sj = h * R_UNITS, h * R_PROJ + (CR + p0), h * R_SCORE + (CR + s0)
                for i in range(4):
                    unit_ready(n + i)
                    for th in range(2):
                        project(i, th, th, pj + (2 * i + th - 1))
                def project_v(b):
                    pe.wait_ge(proj_free, pj + (8 + b - 1))
                    for k in range(KT):
                        if b == 0 and k % 2 == 0:
                            unit_ready(n + (4 + k // 2))
                        mm = mm3(proj_bank[b % 2][:, :], cut(hT, k, part(b)), wslot(k // 2, part(k % 2, HALF)),
                                 k == 0, k == KT - 1)
                    mm.then_inc(proj_done, 1)
                for th in range(2):
                    def scores(b, th=th):
                        j = 9 * th + b
                        if th == 0 and b == 0:
                            pe.wait_ge(proj_free, pj + 8)
                        pe.wait_ge(score_free, sj + (j - 1))
                        for k in range(2):
                            mm = mm3(score_bank[j % 2][:, :], cut(r_kT, k, part(b)), cut(r_qT, k, part(th, HALF)),
                                     k == 0, k == 1)
                        mm.then_inc(score_done, 1)

                    def values(b):
                        if th == 0 and b == 0:
                            pe.wait_ge(proj_free, pj + 16)
                        pe.wait_ge(aT_ready, h * 16 + (CR + 8 * th + b + 1))
                        for dt in range(4):
                            if b == 0:
                                pe.wait_ge(out_free, h * 8 + (CR + o0 + 4 * th + dt - 3))
                            mm = mm3(out_bank[dt][:, :], cut(r_v, b, part(dt)), cut(r_aT, b % 2), b == 0, b == TB - 1)
                            if b == TB - 1:
                                mm.then_inc(out_done, 1)
                        if b < TB - 1:
                            mm.then_inc(pv_done, 1)
                    if th == 0:
                        for b in range(TB - 1):
                            project_v(b)
                        scores(0)
                        project_v(TB - 1)
                    for b in range(TB):
                        if b + 1 < TB:
                            scores(b + 1)
                        values(b)

                    def gate(dt):
                        i = 8 + 4 * th + dt
                        unit_ready(n + i)
                        project(i % WS, th, dt % 2, pj + (16 + 4 * th + dt - 1))
                    gate(0)
                    j = 9 * th + 8
                    pe.wait_ge(sq_sum, h * 2 + (th + 1))
                    pe.wait_ge(score_free, sj + (j - 1))
                    pe.matmul(score_bank[j % 2][:, :], ones[:, :], r_am[:, 0, :], start=True, stop=True) \
                      .then_inc(score_done, 1)
                    for dt in range(1, 4):
                        if th == 0 and dt == 3:
                            scores(0, th=1)
                        gate(dt)

            def out_tile(parts, first_job, j, tb, begin=True, end=True):
                if begin:
                    pe.wait_ge(out_free, first_job + (j - 3))
                for i, (par, slot) in enumerate(parts):
                    for k in range(2):
                        mm = mm3(out_bank[j % 4][:, :], cut(aT, par, k, part(tb)), wslot(slot + k, part(j % 2, HALF)),
                                 begin and i + k == 0, end and k == 1 and i == len(parts) - 1)
                if end:
                    mm.then_inc(out_done, 1)

            def out_group(par, slot, first_job):
                for j in range(G_OUT):
                    out_tile([(par, slot)], first_job, j, j // 2)

            def tail(phase, first_job, last_ready, hidden=None):
                more = phase != "E4"
                for j in range(2 * LONE):
                    out_tile([(0, 0)], first_job, j, TB - LONE + j // 2)
                for j in range(4):
                    out_tile([(0, 0)], first_job, 2 * LONE + j, j // 2, end=False)
                last_ready()
                for j in range(4):
                    out_tile([(1, 2)], first_job, 2 * LONE + j, j // 2, begin=False)
                for tb in range(2, TB):
                    parts = [(0, 0), (1, 2)] if tb < TB - LONE else [(1, 2)]
                    out_tile(parts, first_job, 2 * (LONE + tb), tb)
                    if more and tb >= 3:
                        transpose_norm(phase, tb - 3)
                    out_tile(parts, first_job, 2 * (LONE + tb) + 1, tb)
                if more:
                    if hidden:
                        hT_ready(phase, 1)
                        hidden(0)
                    transpose_norm(phase, TB - 3)
                    if hidden:
                        hidden(1)
                    transpose_norm(phase, TB - 2)
                    transpose_norm(phase, TB - 1)

            def outputs(phase, groups, after, hidden):
                n0, _, _, o0, _ = BASE[phase]
                with pe.Fori(0, groups // 2 - 1) as i:
                    for par in range(2):
                        unit_ready(i * (2 * G_UNITS) + (n0 + G_UNITS * par + 3))
                        out_group(par, 2 * par, i * (2 * G_OUT) + (CR + o0 + G_OUT * par))
                unit_ready(n0 + G_UNITS * (groups - 2) + 3)
                tail(after, CR + o0 + G_OUT * (groups - 2), lambda: unit_ready(n0 + G_UNITS * (groups - 1) + 3), hidden)

            def first_hidden(phase):
                n0, p0 = BASE[phase][:2]

                def job(u):
                    unit_ready(n0 + u)
                    project(u, 0, u, CR + p0 + u - 1)
                return job

            def mlp(phase, before, after):
                n0, p0, _, o0, f0 = BASE[phase]

                def up(g, slot, unit, halves=(0, 1)):
                    for th in halves:
                        for u in range(2):
                            if th == 0:
                                unit_ready(unit + u)
                            project(slot + u, th, u, g * M_PROJ + (CR + p0 + 2 * th + u - 1))

                def ready(g, unit):
                    unit_ready(unit)
                    pe.wait_ge(ff_ready, g * M_PROJ + (f0 + M_PROJ))
                up(0, 0, n0, halves=(1,))
                with pe.Fori(0, N_M // 2 - 1) as i:
                    for par in range(2):
                        g = i * 2 + par
                        up(g + 1, 2, g * G_UNITS + (n0 + 2))
                        ready(g, g * G_UNITS + (n0 + 5))
                        out_group(par, 0, g * G_OUT + (CR + o0))
                g = N_M - 2
                up(g + 1, 2, n0 + 2 + g * G_UNITS)
                ready(g, n0 + 5 + g * G_UNITS)
                tail(after, CR + o0 + g * G_OUT, lambda: ready(g + 1, n0 + 3 + (g + 1) * G_UNITS))

            outputs("O0", N_O0, "E1", first_hidden("M0"))
            hT_ready("E1", 2)
            mlp("M0", "E1", "E2")
            hT_ready("E2", 2)

            n0, p0, s0, _, _ = BASE["A"]
            with pe.Fori(0, 2) as gp:
                n, pj, sj = gp * A_UNITS + n0, gp * A_PROJ + (CR + p0), gp * A_SCORE + (CR + s0)
                for i in range(5):
                    unit_ready(n + i)
                    for th in range(2):
                        project(i % WS, th, th, pj + (2 * i + th - 1))
                unit_ready(n + 5)
                for b in range(TB):
                    pe.wait_ge(proj_free, pj + (10 + b - 1))
                    for k in range(KT):
                        mm = mm3(proj_bank[b % 2][:, 0:P], cut(hT, k, part(b)), wslot(1, part(k)), k == 0, k == KT - 1)
                    mm.then_inc(proj_done, 1)
                pe.wait_ge(proj_free, pj + 18)
                starts = [sum(len(A_BLOCKS[c // 2]) for c in range(r)) for r in range(A_CORE)]

                def scores(c, head):
                    b, two = c // 2, c % 2
                    blocks, j = A_BLOCKS[b], 4 * c + head
                    rows = slice(HD * two, HD * two + HD)
                    pe.wait_ge(score_free, sj + (j - 3))
                    q = [t[rows, head, part(b)] for t in a_qT]
                    k = [t[rows, blocks[0] * P:(blocks[-1] + 1) * P] for t in a_kT]
                    mm3(attn_score_bank[j % 4][:, 0:len(blocks) * P], q, k, True, True).then_inc(score_done, 1)

                def turn(c, i):
                    if i == 0:
                        pe.wait_ge(p_ready, gp * A_CORE + (CR + c + 1))
                    j = 18 + starts[c] + i
                    pe.wait_ge(proj_free, pj + (j - 1))
                    for head in range(4):
                        mm = pe.transpose(proj_bank[j % 2][:, part(head)],
                                          a_s[:, c % 4, head, 1 + i * P:1 + (i + 1) * P], ident[:, :])
                    mm.then_inc(proj_done, 1)

                def values(c, i):
                    blocks, d = A_BLOCKS[c // 2], starts[c] + i
                    if i == 0:
                        pe.wait_ge(attn_free, gp * A_CORE + (CR + c - 1))
                    pe.wait_ge(proj_free, pj + (18 + d + 1))
                    mm3(out_bank[c % 2][:, :], cut(a_v, blocks[i], slice(None)), cut(a_pT, d % A_PT_SLOTS),
                        i == 0, i == len(blocks) - 1).then_inc(attn_done, 1)

                for st in range(A_CORE + 4):
                    for what, i in (("t", 0), ("s", 0), ("s", 1), ("v", 0), ("t", 1), ("s", 2), ("v", 1), ("t", 2),
                                    ("s", 3), ("v", 2)):
                        c = st - {"s": 0, "t": 3, "v": 4}[what]
                        if 0 <= c < A_CORE and (what == "s" or i < len(A_BLOCKS[c // 2])):
                            {"s": scores, "t": turn, "v": values}[what](c, i)

            pe.wait_ge(attn_free, CR + 2 * A_CORE)
            outputs("O1", N_O1, "E3", first_hidden("M1"))
            hT_ready("E3", 2)
            mlp("M1", "E3", "E4")

        @block.scalar
        def _(act):
            step = Steps(act, act_step)
            x_loads, x_stores = [0] * 3, [0] * 3


            def load_x(e, tb):
                s = tb % 3
                if x_stores[s]:
                    act.wait_ge(x_stored[s], 16 * x_stores[s])
                act.dma_start(xt[:, s, :], x_in[e][part(tb), :]).then_inc(x_loaded[s], 16)
                x_loads[s] += 1

            def norm(e):
                phase = f"E{e}"
                s0, o0 = BASE[phase][2], BASE[phase][3]
                load_x(e, 0)
                for i, g in enumerate((post[e], pre[e])):
                    if g is not None:
                        act.dma_start((gain_post, gain_pre)[i][:, :], g.partition_broadcast(P)).then_inc(gains_loaded, 16)
                load_x(e, 1)
                if e == 0:
                    act.dma_start(decay[:, 0, :], log_decay_fwd[0].partition_broadcast(P)).then_inc(params, 16)
                    act.dma_start(decay[:, 1, :], log_decay_bwd[0].partition_broadcast(P)).then_inc(params, 16)
                    act.dma_start(sink[:, :], sink_logits[0].partition_broadcast(P)).then_inc(params, 16)
                for st in range(TB + 3):
                    tb = st - 3
                    if e < 4 and 0 <= tb < TB:
                        for j in range(2):
                            act.wait_ge(score_done, CR + s0 + 2 * tb + j + 1)
                            act.activation(hT[0][:, 4 * j:4 * j + 4, part(tb)],
                                           score_bank[j][:, :].rearrange("p (k t) -> p k t", k=4), ACT.Copy) \
                               .then_inc(hT_hi_ready, 1)
                    tb = st
                    if e and tb < TB:
                        act.wait_ge(out_free, CR + o0 - 16 + 2 * (tb + 1))
                        step(act.activation(squares, y[:, tb, :], ACT.Square, scale=D ** -0.5,
                                            accum_out=stats[:, 0, tb:tb + 1]))
                        act.activation(stats[:, 1, tb:tb + 1], stats[:, 0, tb:tb + 1], ACT.Sqrt, bias=eps_t[:, :]) \
                           .then_inc(std_y, 1)
                    tb = st - 1
                    if 0 <= tb < TB:
                        if e:
                            act.wait_ge(x_new, (e - 1) * TB + tb + 1)
                            act.dma_start(x_out[e][part(tb), :], xt[:, tb % 3, :]).then_inc(x_stored[tb % 3], 16)
                            x_stores[tb % 3] += 1
                        else:
                            act.wait_ge(x_loaded[tb % 3], 16 * (tb // 3 + 1))
                            if tb == 0:
                                act.wait_ge(consts, 4)
                        if e < 4:
                            step(act.activation(squares, xt[:, tb % 3, :], ACT.Square, scale=D ** -0.5,
                                                accum_out=stats[:, 2, tb:tb + 1]))
                            act.activation(stats[:, 3, tb:tb + 1], stats[:, 2, tb:tb + 1], ACT.Sqrt, bias=eps_t[:, :]) \
                               .then_inc(std_x, 1)
                    if 1 <= st < TB - 1:
                        if e < 4 and st >= 2:
                            act.wait_ge(xn_ready, e * TB + st - 1)
                        load_x(e, st + 1)
                if e:
                    for s in range(3):
                        act.wait_ge(x_stored[s], 16 * x_stores[s])

            norm(0)

            _, p0, s0, o0, _ = BASE["R"]
            with act.Fori(0, RH) as h:
                pj, sj = h * R_PROJ + (CR + p0), h * R_SCORE + (CR + s0)

                def hi(j, dst, scale=1.0):
                    act.wait_ge(proj_done, pj + (j + 1))
                    act.activation(dst, proj_bank[j % 2][:, :], ACT.Copy, scale=scale).then_inc(proj_hi, 1)
                for j in range(8):
                    dst, u, th = (r_qT, r_kT)[j // 4], j // 2 % 2, j % 2
                    hi(j, dst[0][:, u, part(th, HALF)], 1.0 if j < 4 else DK ** -0.5)
                def masked_hi(th, b):
                    act.wait_ge(score_free, sj + (9 * th + b + 1))
                    if b >= 2:
                        act.wait_ge(pv_done, h * 14 + (CR + 7 * th + b - 1))
                    else:
                        act.wait_ge(out_done, h * 8 + (CR + 4 * th))
                    act.activation(r_aT[0][:, b % 2, :], r_am[:, b % 2, :], ACT.Copy).then_inc(aT_hi_ready, 1)
                for b in range(TB):
                    if b == TB - 1:
                        masked_hi(0, 0)
                    hi(8 + b, r_v[0][:, b, :])
                    if b == 1:
                        act.wait_ge(mask_ready, h * 4 + 4)
                        act.activation(mask[:, :], mask[:, :], ACT.Exp).then_inc(mask_exp, 1)
                for th in range(2):
                    for b in range(1, TB):
                        masked_hi(th, b)
                    act.wait_ge(aT_ready, h * 16 + (CR + 8 * th + 8))
                    for dt, dst in enumerate((r_am[:, 0, :], r_am[:, 1, :], r_e[:, :], r_sd[:, :])):
                        act.wait_ge(out_done, h * 8 + (CR + 4 * th + dt + 1))
                        act.activation(dst, out_bank[dt][:, :], ACT.Square).then_inc(sq_out, 1)
                    for dt in range(4):
                        act.wait_ge(mix_stored[dt], h * 32 + (16 + 16 * th))
                        act.activation(r_os[:, dt, :], out_bank[dt][:, :], ACT.Copy).then_inc(out_free, 1)
                    for dt in range(4):
                        if th == 0 and dt == 3:
                            masked_hi(1, 0)
                        j = 16 + 4 * th + dt
                        if dt == 0:
                            act.wait_ge(sq_sum, h * 2 + (th + 1))
                        act.wait_ge(proj_done, pj + (j + 1))
                        act.activation(r_e[:, :], proj_bank[j % 2][:, :], ACT.Sigmoid).then_inc(e_ready, 1)
                        if dt == 0:
                            act.wait_ge(score_done, sj + (9 * th + 9))
                            act.activation(r_sd[:, :], score_bank[(9 * th + 8) % 2][:, :], ACT.Sqrt, bias=eps_t[:, :],
                                           scale=1.0 / DV).then_inc(score_free, 1)
                        act.wait_ge(gated, h * 8 + (4 * th + dt + 1))
                        act.dma_start(mix[bass.ds(h * DV + dt * P, P), part(th, HALF)], r_os[:, dt, :]) \
                           .then_inc(mix_stored[dt], 16)

            def mlp(phase):
                _, p0, _, o0, f0 = BASE[phase]

                def group(g, par):
                    for j in range(4):
                        th, u = j // 2, j % 2
                        act.wait_ge(sq_ready, g * M_PROJ + (f0 + CR + j - 1))
                        act.wait_ge(proj_done, g * M_PROJ + (CR + p0 + j + 1))
                        act.activation(relu[:, j % 2, :], proj_bank[j % 2][:, :], ACT.Relu).then_inc(proj_free, 1)
                        if j == 0:
                            act.wait_ge(out_done, g * G_OUT + (CR + o0 - G_OUT))
                        act.wait_ge(proj_free, g * M_PROJ + (CR + p0 + j + 1))
                        act.activation(aT[0][:, par, u, part(th, HALF)], relu[:, j % 2, :], ACT.Square).then_inc(ff_hi, 1)
                group(0, 0)
                with act.Fori(0, N_M // 2 - 1) as i:
                    group(i * 2 + 1, 1)
                    group(i * 2 + 2, 0)
                group(N_M - 1, 1)

            def cut_hi(phase, groups, first_waits):
                n0, _, _, o0, _ = BASE[phase]
                loaded0 = loads_before(phase)

                def unit(i, par, u):
                    act.wait_ge(raw_loaded[u % RAW], i * 64 + (loaded0 + 32 * par + 16 * (u // RAW + 1)))
                    act.activation(output_slot(phase, par, u)[0], w_raw[:, u % RAW, :], ACT.Copy).then_inc(unit_hi_scalar, 1)
                for u in range(4):
                    act.wait_ge(*first_waits[u])
                    unit(0, 1, u)
                with act.Fori(1, groups // 2) as i:
                    for par in range(2):
                        act.wait_ge(out_done, i * (2 * G_OUT) + (CR + o0 + G_OUT * (par - 1)))
                        for u in range(4):
                            unit(i, par, u)

            p_end = CR + RH * R_PROJ
            scores_read = (score_done, CR + BASE["R"][2] + RH * R_SCORE - 1)
            cut_hi("O0", N_O0, [scores_read, scores_read, (proj_done, p_end - 1), (proj_done, p_end)])
            norm(1)
            mlp("M0")
            norm(2)

            _, p0, s0, _, _ = BASE["A"]
            with act.Fori(0, 2) as gp:
                pj, cj = gp * A_PROJ + (CR + p0), gp * A_CORE
                for j in range(18):
                    act.wait_ge(proj_done, pj + (j + 1))
                    src = proj_bank[j % 2]
                    if j < 8:
                        act.activation(a_qT[0][:, j // 2, part(j % 2, HALF)], src[:, :], ACT.Copy, scale=HD ** -0.5) \
                           .then_inc(proj_hi, 1)
                    elif j < 10:
                        act.activation(a_kT[0][:, part(j % 2, HALF)], src[:, :], ACT.Copy).then_inc(proj_hi, 1)
                    else:
                        act.activation(a_v[0][:, j - 10, :], src[:, 0:P], ACT.Copy).then_inc(proj_hi, 1)
                done = 0
                ends = [0]
                for st in range(A_CORE + 5):
                    for i in range(4):
                        c = st - 3
                        if 0 <= c < A_CORE and i < len(A_BLOCKS[c // 2]):
                            j = 18 + done
                            act.wait_ge(attn_done, gp * A_PT + (CR + done - A_PT_SLOTS + 1))
                            act.wait_ge(proj_done, pj + (j + 1))
                            act.activation(a_pT[0][:, done % A_PT_SLOTS, :], proj_bank[j % 2][:, :], ACT.Copy) \
                               .then_inc(proj_hi, 1)
                            done += 1
                            if i == len(A_BLOCKS[c // 2]) - 1:
                                ends.append(done)
                        c = st - 5
                        if 0 <= c < A_CORE and i == 0:
                            b, two = c // 2, c % 2
                            rows = slice(HD * two, HD * two + HD)
                            act.wait_ge(attn_done, gp * A_PT + (CR + ends[c + 1]))
                            act.wait_ge(attn_out[c % 2], gp * (8 * A_CORE) + 16 * (1 + c // 2))
                            act.activation(a_out[rows, c % 2, :], out_bank[c % 2][rows, :], ACT.Copy) \
                               .then_inc(attn_free, 1)
                            act.wait_ge(attn_free, cj + (CR + c + 1))
                            act.dma_start(mix[bass.ds(gp * (8 * HD) + 4 * HD * two, 4 * HD), part(b)]
                                          .rearrange("(j d) t -> d j t", d=HD),
                                          a_out[rows, c % 2, :].rearrange("d (j t) -> d j t", j=4)) \
                               .then_inc(attn_out[c % 2], 16)
                        c = st - 1
                        if 0 <= c < A_CORE:
                            if i == 0:
                                act.wait_ge(max_ready, cj + (c + 1))
                            s = a_s[:, c % 4, i, 0:1 + len(A_BLOCKS[c // 2]) * P]
                            ins = act.activation(s, s, ACT.Exp, bias=nmax[:, c % 2, i:i + 1],
                                                 accum_out=row_sum[:, c % 2, i:i + 1])
                            if i == 3:
                                ins.then_inc(exp_ready, 1)
            for s in attn_out:
                act.wait_ge(s, ATTN_STORES)
            q_read = (proj_done, CR + p0 + A_PROJ + 18)
            scores_read = (score_done, CR + s0 + 2 * A_SCORE)
            cut_hi("O1", N_O1, [q_read, q_read, scores_read, scores_read])
            norm(3)
            mlp("M1")
            norm(4)

        @block.vector
        def _(dve):
            step = Steps(dve, dve_step)
            gains = [0]

            def minus(dst, src, hi, scale=None):
                if scale is None:
                    return dve.tensor_tensor(dst, src, hi.bitcast(f32), ALU.subtract)
                return dve.scalar_tensor_tensor(out=dst, in0=src, scalar=scale, in1=hi.bitcast(f32), op0=ALU.mult,
                                                op1=ALU.subtract)

            def add_tile(first_job, j, tb, first=False):
                dst, src = y[:, tb, part(j % 2, HALF)], out_bank[j % 4][:, :]
                dve.wait_ge(out_done, first_job + (j + 1))
                if first:
                    dve.tensor_copy(dst, src).then_inc(out_free, 1)
                else:
                    dve.tensor_tensor(dst, dst, src, ALU.add).then_inc(out_free, 1)

            def add_group(first_job, first=False):
                dve.wait_ge(out_free, first_job)
                for j in range(G_OUT):
                    add_tile(first_job, j, j // 2, first)

            def norm(e):
                phase = f"E{e}"
                s0, o0 = BASE[phase][2], BASE[phase][3]
                tail = CR + o0 - TAIL
                gains[0] += 16 * ((post[e] is not None) + (pre[e] is not None))
                if e:
                    dve.wait_ge(out_free, tail)
                    for j in range(2 * LONE):
                        add_tile(tail, j, TB - LONE + j // 2)
                    dve.wait_ge(out_free, tail + 2 * LONE)
                for st in range(TB + 3):
                    tb = st
                    if e and tb < TB:
                        add_tile(tail, 2 * (LONE + tb), tb)
                        add_tile(tail, 2 * (LONE + tb) + 1, tb)
                    tb = st - 3
                    if e < 4 and 0 <= tb < TB:
                        for j in range(2):
                            dve.wait_ge(hT_hi_ready, e * 2 * TB + 2 * tb + j + 1)
                            four = slice(4 * j, 4 * j + 4)
                            minus(hT[1][:, four, part(tb)], score_bank[j][:, :].rearrange("p (k t) -> p k t", k=4),
                                  hT[0][:, four, part(tb)]).then_inc(score_free, 1)
                    tb = st
                    if e and tb < TB:
                        dve.wait_ge(std_y, (e - 1) * TB + tb + 1)
                        step(dve.reciprocal(stats[:, 4, tb:tb + 1], stats[:, 1, tb:tb + 1]))
                        if tb == 0:
                            dve.wait_ge(gains_loaded, gains[0])
                        dve.scalar_tensor_tensor(out=y[:, tb, :], in0=y[:, tb, :], scalar=stats[:, 4, tb:tb + 1],
                                                 in1=gain_post[:, :], op0=ALU.mult, op1=ALU.mult).then_inc(z_ready, 1)
                    tb = st - 1
                    if e < 4 and 0 <= tb < TB:
                        dve.wait_ge(std_x, e * TB + tb + 1)
                        step(dve.reciprocal(stats[:, 5, tb:tb + 1], stats[:, 3, tb:tb + 1]))
                        if e == 0 and tb == 0:
                            dve.wait_ge(gains_loaded, gains[0])
                        dve.scalar_tensor_tensor(out=xn[:, tb % 2, :], in0=xt[:, tb % 3, :],
                                                 scalar=stats[:, 5, tb:tb + 1], in1=gain_pre[:, :], op0=ALU.mult,
                                                 op1=ALU.mult).then_inc(xn_ready, 1)

            norm(0)
            dve.wait_ge(consts, 6 + AH)
            dve.tensor_copy(dist16[:, :], dist_i[:, :])
            dve.wait_ge(params, 48)
            step(dve.tensor_scalar(decay[:, 1, :], decay[:, 1, :], -1.0, None, ALU.mult))

            _, p0, s0, o0, _ = BASE["R"]
            PIECE = MASK // 4
            with dve.Fori(0, RH) as h:
                step.enter(h, 1 + 4 + 2 * (1 + 1 + 4))
                pj, sj = h * R_PROJ + (CR + p0), h * R_SCORE + (CR + s0)
                step(dve.tensor_copy(decay_now[:, :].unsqueeze(2), decay[:, :, bass.ds(h, 1)]))
                for j in range(8):
                    pair, u, th = (r_qT, r_kT)[j // 4], j // 2 % 2, j % 2
                    dve.wait_ge(proj_hi, h * 16 + (j + 1))
                    dst = cut(pair, u, part(th, HALF))
                    minus(dst[1], proj_bank[j % 2][:, :], dst[0], None if j < 4 else DK ** -0.5).then_inc(proj_free, 1)
                    if j >= 4:
                        m = slice((j - 4) * PIECE, (j - 3) * PIECE)
                        tmp = r_am[:, 0, 0:PIECE]
                        dve.tensor_scalar(mask[:, m], dist16[:, m], 0.0, decay_now[:, 0:1], ALU.max, ALU.mult)
                        step(dve.tensor_scalar(tmp, dist16[:, m], 0.0, decay_now[:, 1:2], ALU.min, ALU.mult))
                        ins = dve.tensor_tensor(mask[:, m], mask[:, m], tmp, ALU.add)
                        ins.then_inc(mask_ready, 1)
                        dve.wait_ge(mask_ready, h * 4 + (j - 3))
                def masked(th, b):
                    j = 8 * th + b
                    dve.wait_ge(aT_hi_ready, h * 16 + (CR + j - 1))
                    dve.wait_ge(score_done, sj + (9 * th + b + 1))
                    at = th * HALF + (TB - 1 - b) * P
                    dve.tensor_tensor(r_am[:, b % 2, :], score_bank[(9 * th + b) % 2][:, :], mask[:, at:at + HALF],
                                      ALU.mult).then_inc(score_free, 1)
                    dve.wait_ge(aT_hi_ready, h * 16 + (CR + j + 1))
                    minus(r_aT[1][:, b % 2, :], r_am[:, b % 2, :], r_aT[0][:, b % 2, :]).then_inc(aT_ready, 1)
                for b in range(TB):
                    if b == TB - 1:
                        dve.wait_ge(mask_exp, h + 1)
                        masked(0, 0)
                    dve.wait_ge(proj_hi, h * 16 + (9 + b))
                    minus(r_v[1][:, b, :], proj_bank[b % 2][:, :], r_v[0][:, b, :]).then_inc(proj_free, 1)
                for th in range(2):
                    for b in range(1, TB):
                        masked(th, b)
                    dve.wait_ge(sq_out, h * 8 + (4 * th + 4))
                    dve.tensor_tensor(r_am[:, 0, :], r_am[:, 0, :], r_am[:, 1, :], ALU.add)
                    step(dve.tensor_tensor(r_e[:, :], r_e[:, :], r_sd[:, :], ALU.add))
                    dve.tensor_tensor(r_am[:, 0, :], r_am[:, 0, :], r_e[:, :], ALU.add).then_inc(sq_sum, 1)
                    for dt in range(4):
                        if th == 0 and dt == 3:
                            masked(1, 0)
                        j = 16 + 4 * th + dt
                        dve.wait_ge(e_ready, h * 8 + (4 * th + dt + 1))
                        dve.tensor_tensor(r_os[:, dt, :], r_os[:, dt, :], proj_bank[j % 2][:, :], ALU.mult) \
                           .then_inc(proj_free, 1)
                        if dt == 0:
                            dve.wait_ge(score_free, sj + (9 * th + 9))
                            step(dve.reciprocal(r_sd[:, :], r_sd[:, :]))
                        dve.wait_ge(proj_free, pj + (j + 1))
                        step(dve.tensor_tensor(r_os[:, dt, :], r_os[:, dt, :], r_sd[:, :], ALU.mult))
                        dve.tensor_tensor(r_os[:, dt, :], r_os[:, dt, :], r_e[:, :], ALU.mult).then_inc(gated, 1)
            step.leave(RH)

            def outputs(phase, groups):
                o0 = BASE[phase][3]
                add_group(CR + o0, first=True)
                with dve.Fori(1, groups - 2) as g:
                    add_group(g * G_OUT + (CR + o0))

            def mlp(phase):
                _, p0, _, o0, f0 = BASE[phase]

                def hidden(g, par):
                    for j in range(4):
                        th, u = j // 2, j % 2
                        dve.wait_ge(proj_free, g * M_PROJ + (CR + p0 + j + 1))
                        r = relu[:, j % 2, :]
                        dve.tensor_tensor(relu_sq[:, j % 2, :], r, r, ALU.mult).then_inc(sq_ready, 1)
                        dve.wait_ge(sq_ready, g * M_PROJ + (f0 + CR + j + 1))
                        dve.wait_ge(ff_hi, g * M_PROJ + (f0 + j + 1))
                        dst = cut(aT, par, u, part(th, HALF))
                        minus(dst[1], relu_sq[:, j % 2, :], dst[0]).then_inc(ff_ready, 1)
                hidden(0, 0)
                hidden(1, 1)
                add_group(CR + o0, first=True)
                with dve.Fori(0, N_M // 2 - 2) as i:
                    for par in range(2):
                        g = i * 2 + (1 + par)
                        hidden(g + 1, par)
                        add_group(g * G_OUT + (CR + o0))
                g = N_M - 3
                hidden(g + 1, 0)
                add_group(g * G_OUT + (CR + o0))
                hidden(g + 2, 1)

            outputs("O0", N_O0)
            norm(1)
            mlp("M0")
            norm(2)

            _, p0, s0, _, _ = BASE["A"]
            h0 = 16 * RH
            step(dve.tensor_copy(a_dist[:, :], a_iota[:, :]))
            step(dve.tensor_scalar(a_far[:, :], a_dist[:, :], -1.0, None, ALU.mult))
            step(dve.tensor_tensor(a_dist[:, :], a_dist[:, :], a_far[:, :], ALU.max))
            step(dve.tensor_scalar(a_far[:, :], a_dist[:, :], float(P), BIG, ALU.is_gt, ALU.mult))
            step(dve.tensor_tensor(a_dist[:, :], a_dist[:, :], a_far[:, :], ALU.add))
            with dve.Fori(0, 2) as gp:
                step.enter(gp, 1)
                pj, sj, cj = gp * A_PROJ + (CR + p0), gp * A_SCORE + (CR + s0), gp * A_CORE
                dve.tensor_copy(slope_now[:, :], slope[:, bass.ds(gp * 8, 8)])
                step(dve.tensor_copy(sink_now[:, :], sink[:, bass.ds(gp * 8, 8)]))
                for j in range(18):
                    dve.wait_ge(proj_hi, gp * A_PROJ + (h0 + j + 1))
                    src = proj_bank[j % 2]
                    if j < 8:
                        dst = cut(a_qT, j // 2, part(j % 2, HALF))
                        minus(dst[1], src[:, :], dst[0], HD ** -0.5).then_inc(proj_free, 1)
                    elif j < 10:
                        dst = cut(a_kT, part(j % 2, HALF))
                        minus(dst[1], src[:, :], dst[0]).then_inc(proj_free, 1)
                    else:
                        dst = cut(a_v, j - 10, slice(None))
                        minus(dst[1], src[:, 0:P], dst[0]).then_inc(proj_free, 1)
                done = 0
                for st in range(A_CORE + 3):
                    if st < A_CORE:
                        b, two = st // 2, st % 2
                        blocks = A_BLOCKS[b]
                        nk, left = len(blocks) * P, (blocks[0] - b + 1) * P
                        dve.tensor_copy(a_s[:, st % 4, :, 0:1], sink_now[:, 4 * two:4 * two + 4].unsqueeze(2))
                    for head in range(4):
                        if st < A_CORE:
                            dve.wait_ge(score_done, sj + (4 * st + head + 1))
                            dve.scalar_tensor_tensor(out=a_s[:, st % 4, head, 1:1 + nk], in0=a_dist[:, left:left + nk],
                                                     scalar=slope_now[:, 4 * two + head:4 * two + head + 1],
                                                     in1=attn_score_bank[head][:, 0:nk], op0=ALU.mult, op1=ALU.add) \
                               .then_inc(score_free, 1)
                        c = st - 3
                        if c >= 0 and head < len(A_BLOCKS[c // 2]):
                            dve.wait_ge(proj_hi, gp * A_PROJ + (h0 + 18 + done + 1))
                            dst = cut(a_pT, done % A_PT_SLOTS)
                            minus(dst[1], proj_bank[done % 2][:, :], dst[0]).then_inc(proj_free, 1)
                            done += 1
                    if st < A_CORE:
                        dve.wait_ge(score_free, sj + (4 * st + 4))
                        dve.tensor_reduce(nmax[:, st % 2, :], a_s[:, st % 4, :, 0:1 + nk], AX.X, ALU.max, negate=True) \
                           .then_inc(max_ready, 1)
                    c = st - 1
                    if 0 <= c < A_CORE:
                        dve.wait_ge(exp_ready, cj + (c + 1))
                        dve.reciprocal(row_inv[:, c % 2, :], row_sum[:, c % 2, :]).then_inc(inv_ready, 1)
            step.leave(2)

            outputs("O1", N_O1)
            norm(3)
            mlp("M1")
            norm(4)


_INS = ["x", "w_in_ret", "w_out_ret", "log_decay_fwd", "log_decay_bwd", "w_in_attn", "w_out_attn", "sink_logits",
        "g_pre_mix", "g_post_mix", "g_pre_mlp", "g_post_mlp", "w_up", "w_down"]


def kernel(**inputs):
    import numpy as np
    import concourse.bacc as bacc
    from concourse.bass_utils import run_bass_kernel_spmd

    nc = bacc.Bacc("TRN2", target_bir_lowering=False, num_devices=1)
    arrays, args = {}, []
    for name in _INS:
        a = np.ascontiguousarray(inputs[name])
        arrays[f"in_{name}"] = a
        args.append(nc.dram_tensor(f"in_{name}", a.shape, mybir.dt.from_np(a.dtype), kind="ExternalInput").ap())
    args.append(nc.dram_tensor("result", (1, T, D), mybir.dt.float32, kind="ExternalOutput").ap())
    build(nc, *args)
    r = run_bass_kernel_spmd(nc, [arrays], core_ids=[0])
    return r.results[0]["result"]
```

```python
import concourse.bass as bass
from concourse import mybir

P = 128
D = 1024
T = 1024
KT = D // P
TB = T // P
HALF = 512
RH, DK, DV = 4, 256, 512
NQ, NV = RH * DK, RH * DV
AH, AG, HD = 16, 4, 64
FF = 4 * D
EPS = 1e-6
BIG = 1e30

RAW = 2
WS = 4
UNIT = 1024
CR = 4

R_UNITS, R_PROJ, R_SCORE, R_OUT = 16, 24, 18, 8
G_UNITS, G_OUT = 4, 16
LONE = 3
TAIL = G_OUT + 2 * LONE
M_PROJ = 4
V_UNITS, V_PROJ = 2, 4
A_UNITS, A_CORE, A_SCORE = 5, 16, 64
A_BLOCKS = [[kb for kb in (b - 1, b, b + 1) if 0 <= kb < TB] for b in range(TB)]
A_PT = 2 * sum(len(x) for x in A_BLOCKS)
QK_PROJ = 10
A_PROJ = QK_PROJ + A_PT
A_PT_SLOTS = 4
N_O0, N_O1, N_M = NV // (2 * P), D // (2 * P), FF // (2 * P)


def bases():
    unit = proj = score = out = ff = 0
    b = {}

    def at(name):
        b[name] = (unit, proj, score, out, ff)
    at("E0"); score += 16
    at("R"); unit += RH * R_UNITS; proj += RH * R_PROJ; score += RH * R_SCORE; out += RH * R_OUT
    at("O0"); unit += N_O0 * G_UNITS; out += (N_O0 - 2) * G_OUT + TAIL
    at("E1"); score += 16
    at("M0"); unit += N_M * G_UNITS; proj += N_M * M_PROJ; out += (N_M - 2) * G_OUT + TAIL; ff += N_M * M_PROJ
    at("E2"); score += 16
    at("A"); unit += V_UNITS + 2 * A_UNITS; proj += V_PROJ + 2 * A_PROJ; score += 2 * A_SCORE
    at("O1"); unit += N_O1 * G_UNITS; out += (N_O1 - 2) * G_OUT + TAIL
    at("E3"); score += 16
    at("M1"); unit += N_M * G_UNITS; proj += N_M * M_PROJ; out += (N_M - 2) * G_OUT + TAIL; ff += N_M * M_PROJ
    at("E4")
    return b


BASE = bases()


def loads_before(phase, slot):
    return 16 * BASE[phase][0] // RAW + ((80, 48)[slot] if phase in ("O1", "M1") else 0)


class Steps:

    def __init__(self, eng, sem):
        self.eng, self.sem, self.n, self.base = eng, sem, 0, 0

    def __call__(self, ins):
        ins.then_inc(self.sem, 1)
        self.n += 1
        self.eng.wait_ge(self.sem, self.base + self.n)

    def enter(self, i, stride):
        self.start, self.stride, self.base = self.n, stride, i * stride

    def leave(self, rounds):
        assert self.n - self.start == self.stride, (self.n - self.start, self.stride)
        self.n, self.base = self.start + rounds * self.stride, 0


def build(nc, x, w_in_ret, w_out_ret, log_decay_fwd, log_decay_bwd, w_in_attn, w_out_attn, sink_logits,
          g_pre_mix, g_post_mix, g_pre_mlp, g_post_mlp, w_up, w_down, out):
    f32, f32r, f16, i32 = mybir.dt.float32, mybir.dt.float32r, mybir.dt.float16, mybir.dt.int32
    ACT, ALU, AX = mybir.ActivationFunctionType, mybir.AluOpType, mybir.AxisListType

    at = [(nc.sbuf_base + 63) // 64 * 64]

    def sb(name, shape, dt, offset=None):
        size = 4
        for s in shape[1:]:
            size *= s
        size = (size // 2 if dt == f16 else size) + 31 & -32
        if offset is None:
            offset, at[0] = at[0], at[0] + size
        assert offset + size <= nc.sbuf_usable_end, (name, offset + size, nc.sbuf_usable_end)
        return nc.alloc_sbuf_tensor_at(name, shape, dt, offset=offset)

    hT = [sb("hT_hi", [P, KT, T], f32r), sb("hT_lo", [P, KT, T], f32r)]
    w_raw = sb("w_raw", [P, RAW, UNIT], f32)
    w_split = [sb("w_hi", [P, WS, UNIT], f32r), sb("w_lo", [P, WS, UNIT], f32r)]
    ident = sb("ident", [P, P], f32)
    ones = sb("ones", [P, P], f32)
    one = ones[:, 0:1]
    stats = sb("stats", [P, 6, TB], f32)
    eps_t = sb("eps_t", [P, 1], f32)
    table_load = sb("table_load", [P, 1], f32)
    decay = sb("decay", [P, 2, RH], f32)
    decay_now = sb("decay_now", [P, 2], f32)
    slope = sb("slope", [P, AH], f32)
    slope_now = sb("slope_now", [P, 8], f32)
    q_scale = sb("q_scale", [P, AH // 2], f32)
    q_scale_now = sb("q_scale_now", [P, 4], f32)
    sink = sb("sink", [P, AH], f32)
    sink_now = sb("sink_now", [P, 8], f32)
    smax = sb("smax", [P, 2, 4], f32)
    nmax = sb("nmax", [P, 2, 4], f32)
    row_sum = sb("row_sum", [P, 2, 4], f32)
    row_inv = sb("row_inv", [P, 2, 4], f32)
    a_iota = sb("a_iota", [P, 3 * P], i32)
    arena = (at[0] + 63) // 64 * 64

    at[0] = arena
    r_qT = [sb("r_qT_hi", [P, 2, T], f32r), sb("r_qT_lo", [P, 2, T], f32r)]
    r_kT = [sb("r_kT_hi", [P, 2, T], f32r), sb("r_kT_lo", [P, 2, T], f32r)]
    r_v = [sb("r_v_hi", [P, TB, DV], f32r), sb("r_v_lo", [P, TB, DV], f32r)]
    MASK = 2 * T - P
    dist16 = sb("dist16", [P, MASK], f16)
    r_aT = [sb("r_aT_hi", [P, 2, HALF], f32r), sb("r_aT_lo", [P, 2, HALF], f32r)]
    mask = sb("mask", [P, MASK], f32)
    r_am = sb("r_am", [P, 2, HALF], f32)
    r_os = sb("r_os", [P, 4, HALF], f32)
    r_e = sb("r_e", [P, HALF], f32)
    r_sd = sb("r_sd", [P, HALF], f32)

    dist_i = sb("dist_i", [P, MASK], i32, offset=arena + 4 * 8 * T)

    at[0] = arena
    aT = [sb("aT_hi", [P, 2, 2, T], f32r), sb("aT_lo", [P, 2, 2, T], f32r)]
    y = sb("y", [P, TB, D], f32)
    relu = sb("relu", [P, 2, HALF], f32)
    relu_sq = sb("relu_sq", [P, 2, HALF], f32)
    squares = relu_sq[:, :, :].rearrange("p a t -> p (a t)")
    xt = sb("xt", [P, 3, D], f32)
    xn = sb("xn", [P, 2, D], f32)
    gain_post = sb("gain_post", [P, D], f32)
    gain_pre = sb("gain_pre", [P, D], f32)

    at[0] = arena
    a_vraw = sb("a_vraw", [P, TB, AG * HD], f32)
    a_qT = [sb("a_qT_hi", [P, 4, T], f32r), sb("a_qT_lo", [P, 4, T], f32r)]
    a_kT = [sb("a_kT_hi", [P, T], f32r), sb("a_kT_lo", [P, T], f32r)]
    a_v = [sb("a_v_hi", [P, TB, P], f32r), sb("a_v_lo", [P, TB, P], f32r)]
    a_pT = [sb("a_pT_hi", [P, A_PT_SLOTS, HALF], f32r), sb("a_pT_lo", [P, A_PT_SLOTS, HALF], f32r)]
    a_s = sb("a_s", [P, 4, 4, 1 + 3 * P], f32)
    a_out = sb("a_out", [P, HALF], f32)
    a_dist = sb("a_dist", [P, 3 * P], f32)
    a_far = a_out[:, 0:3 * P]

    banks = [nc.alloc_psum_tensor(f"bank{i}", [P, HALF], f32) for i in range(8)]
    score_bank, proj_bank, out_bank = banks[0:2], banks[2:4], banks[4:8]
    attn_score_bank = banks[0:2] + banks[6:8]

    mix = nc.dram_tensor("mix", (NV, T), f32).ap()
    x_mid = [nc.dram_tensor(f"x_mid{i}", (T, D), f32).ap() for i in range(3)]
    x_in = [x[0], x[0], x_mid[0], x_mid[1], x_mid[2]]
    x_out = [None, x_mid[0], x_mid[1], x_mid[2], out[0]]
    post = [None, g_post_mix[0], g_post_mlp[0], g_post_mix[1], g_post_mlp[1]]
    pre = [g_pre_mix[0], g_pre_mlp[0], g_pre_mix[1], g_pre_mlp[1], None]

    sem = nc.alloc_semaphore
    raw_loaded = [sem(f"raw_loaded{i}") for i in range(RAW)]
    unit_hi = sem("unit_hi")
    unit_hi_scalar = sem("unit_hi_scalar")
    unit_split = sem("unit_split")
    proj_done, proj_free = sem("proj_done"), sem("proj_free")
    score_done, score_free = sem("score_done"), sem("score_free")
    out_done, out_free = sem("out_done"), sem("out_free")
    proj_hi = sem("proj_hi")
    consts, params = sem("consts"), sem("params")
    act_step, dve_step = sem("act_step"), sem("dve_step")
    gains_loaded = sem("gains_loaded")
    x_loaded = [sem(f"x_loaded{i}") for i in range(3)]
    x_stored = [sem(f"x_stored{i}") for i in range(3)]
    std_y, std_x = sem("std_y"), sem("std_x")
    z_ready = sem("z_ready")
    x_new = sem("x_new")
    xn_ready = sem("xn_ready")
    hT_hi_ready = sem("hT_hi_ready")
    sq_ready = sem("sq_ready")
    ff_hi, ff_ready = sem("ff_hi"), sem("ff_ready")
    mask_ready, mask_exp = sem("mask_ready"), sem("mask_exp")
    aT_hi_ready, aT_ready = sem("aT_hi_ready"), sem("aT_ready")
    pv_done = sem("pv_done")
    sq_out, sq_sum = sem("sq_out"), sem("sq_sum")
    e_ready, gated = sem("e_ready"), sem("gated")
    mix_stored = [sem(f"mix_stored{i}") for i in range(4)]
    scales_ready = sem("scales_ready")
    max_ready, exp_ready = sem("max_ready"), sem("exp_ready")
    inv_ready, p_ready = sem("inv_ready"), sem("p_ready")
    attn_done, attn_free = sem("attn_done"), sem("attn_free")
    attn_out = [sem(f"attn_out{i}") for i in range(2)]
    credited = [unit_split, proj_done, proj_free, score_done, score_free, out_done, out_free,
                aT_hi_ready, aT_ready, pv_done, attn_done, attn_free, p_ready, sq_ready]

    def part(k, n=P):
        return slice(k * n, (k + 1) * n)

    def cut(pair, *idx):
        return [t[(slice(None), *idx)] for t in pair]

    def wslot(s, cols):
        return cut(w_split, s, cols)

    def norm_banks(phase):
        return attn_score_bank if phase == "E0" else score_bank

    def residual_parts(e, tb):
        return [part(i, HALF) for i in range(2)] if (e, tb) == (4, TB - 1) else [slice(0, D)]

    def output_slot(phase, par, u):
        k = u % 2
        return cut(aT, par, k) if (u < 2) == (phase == "O0") else wslot(2 * par + k, slice(None))

    FIRST_CONSTS = 4
    ALL_CONSTS = FIRST_CONSTS + 2 * AH + 2
    ATTN_STORES = 16 * (1 + A_CORE)

    block = nc.Block()
    with block:

        @block.sync
        def _(sp):
            for s in credited:
                sp.sem_inc(s, CR)
            for s in mix_stored + attn_out:
                sp.sem_inc(s, 16)

            def load(n, slot, dst, src):
                sp.wait_ge(unit_split, CR + n - RAW + 1)
                sp.dma_start(dst, src).then_inc(raw_loaded[slot], 16)

            def by_column(slot):
                return w_raw[:, slot, :].rearrange("p (k c) -> p k c", k=KT)

            w_r = w_in_ret[0].rearrange("(k p) c -> p k c", p=P)
            with sp.Fori(0, RH) as h:
                n = h * R_UNITS
                idx = 0
                for c0 in (0, NQ):
                    for u in range(2):
                        load(n + idx, idx % RAW, by_column(idx % RAW), w_r[:, :, bass.ds(h * DK + (c0 + u * P), P)])
                        idx += 1
                for u in range(4):
                    load(n + idx, idx % RAW, w_raw[:, idx % RAW, :].rearrange("p (k c) -> p k c", k=2),
                         w_r[:, 2 * u:2 * u + 2, bass.ds(h * DV + 2 * NQ, DV)])
                    idx += 1
                for th in range(2):
                    for u in range(4):
                        load(n + idx, idx % RAW, by_column(idx % RAW),
                             w_r[:, :, bass.ds(h * DV + (2 * NQ + NV + u * P), P)])
                        idx += 1

            def load_outputs(phase, groups, w, stored, each):
                n0 = BASE[phase][0]
                with sp.Fori(0, groups // 2) as i:
                    stores = sp.snap(i * each + (16 + each))
                    slot_free = sp.snap(i * (2 * G_UNITS) + (n0 + CR - RAW + 1))
                    for st in stored:
                        sp.wait_ge(st, stores)
                    sp.wait_ge(unit_split, slot_free)
                    for par in range(2):
                        n, row = i * (2 * G_UNITS) + (n0 + G_UNITS * par), i * (4 * P) + 2 * P * par
                        sources = (w, mix) if phase == "O1" else (mix, w)
                        for u in range(4):
                            load(n + u, u % RAW, w_raw[:, u % RAW, :], sources[u // 2][bass.ds(row + u % 2 * P, P), :])

            def load_mlp(phase, layer):
                n0 = BASE[phase][0]
                up = w_up[layer].rearrange("(k p) c -> p k c", p=P)
                down = w_down[layer]
                for u in range(2):
                    load(n0 + u, u, by_column(u), up[:, :, part(u)])
                with sp.Fori(0, N_M - 1) as g:
                    for u in range(2):
                        load(g * G_UNITS + (n0 + 2 + u), u, by_column(u),
                             up[:, :, bass.ds(g * (2 * P) + (2 + u) * P, P)])
                    for u in range(2):
                        load(g * G_UNITS + (n0 + 4 + u), u, w_raw[:, u, :], down[bass.ds(g * (2 * P) + u * P, P), :])
                for u in range(2):
                    load(n0 + (N_M - 1) * G_UNITS + 2 + u, u, w_raw[:, u, :], down[part(2 * (N_M - 1) + u), :])

            load_outputs("O0", N_O0, w_out_ret[0], mix_stored, 16 * 2)
            load_mlp("M0", 0)

            wa = w_in_attn[0].rearrange("(k p) c -> p k c", p=P)
            n0 = BASE["A"][0]
            for u in range(V_UNITS):
                load(n0 + u, u, w_raw[:, u, :].rearrange("p (k c) -> p k c", k=4),
                     wa[:, 4 * u:4 * u + 4, (AH + AG) * HD:(AH + 2 * AG) * HD])
            with sp.Fori(0, 2) as gp:
                n = gp * A_UNITS + (n0 + V_UNITS)
                for j in range(4):
                    s = j % RAW
                    sp.wait_ge(unit_split, n + (CR + max(0, j - RAW + 1)))
                    for two in range(2):
                        dst = w_raw[:, s, :].rearrange("p (k two c) -> p k two c", k=KT, two=2)[:, :, two, :]
                        sp.dma_start(dst, wa[:, :, bass.ds(gp * (8 * HD) + (4 * two + j) * HD, HD)]) \
                          .then_inc(raw_loaded[s], 16)
                load(n + 4, 0, by_column(0), wa[:, :, bass.ds(gp * P + AH * HD, P)])

            sp.wait_ge(unit_split, CR + BASE["O1"][0])
            load_outputs("O1", N_O1, w_out_attn[0], attn_out, 16 * A_CORE // 2)
            load_mlp("M1", 1)

        @block.gpsimd
        def _(pool):
            pool.memset(ident[:, :], 0.0).then_inc(consts, 1)
            pool.wait_ge(consts, 1)
            pool.affine_select(out=ident[:, :], in_=ident[:, :], compare_op=ALU.not_equal, fill=1.0, base=0,
                               pattern=[[-1, P]], channel_multiplier=1).then_inc(consts, 1)
            pool.memset(ones[:, :], 1.0).then_inc(consts, 1)
            pool.memset(eps_t[:, :], EPS).then_inc(consts, 1)
            for i in range(AH):
                pool.memset(slope[:, i:i + 1], -2.0 ** (-8.0 * (i + 1) / AH)).then_inc(consts, 1)
            pool.wait_ge(consts, FIRST_CONSTS + AH)
            for two in range(2):
                for gp in range(2):
                    for j in range(4):
                        i = 8 * gp + 4 * two + j
                        pool.memset(q_scale[HD * two:HD * two + HD, 4 * gp + j:4 * gp + j + 1],
                                    -(HD ** -0.5) * 2.0 ** (8.0 * (i + 1) / AH)).then_inc(consts, 1)
                pool.wait_ge(consts, FIRST_CONSTS + AH + 8 * (two + 1))
            pool.iota(dist_i[:, :], pattern=[[1, MASK]], base=-(T - P), channel_multiplier=-1).then_inc(consts, 1)
            pool.iota(a_iota[:, :], pattern=[[1, 3 * P]], base=-P, channel_multiplier=-1).then_inc(consts, 1)
            pool.wait_ge(consts, ALL_CONSTS)

            scalar_units = [0]

            def cut_unit(slot, loaded, dst, n, halves=(0, 1)):
                raw = w_raw[:, slot, :]
                if 0 in halves:
                    pool.wait_ge(raw_loaded[slot], loaded)
                    pool.tensor_tensor(dst[0], raw, one.broadcast_to([P, UNIT]), ALU.mult).then_inc(unit_hi, 1)
                if 1 not in halves:
                    return
                pool.wait_ge(unit_hi, n + (1 - scalar_units[0]))
                pool.tensor_tensor(dst[1], raw, dst[0].bitcast(f32), ALU.subtract).then_inc(unit_split, 1)

            with pool.Fori(0, RH) as h:
                for i in range(R_UNITS):
                    free_at = {0: -3, 1: -2, 2: -1, 3: 0, 4: 2, 5: 4, 6: 6, 7: 8}.get(i, 16 if i < 12 else 17 + i - 12)
                    pool.wait_ge(proj_done, h * R_PROJ + (CR + free_at))
                    cut_unit(i % RAW, h * (16 * R_UNITS // RAW) + 16 * (i // RAW + 1), wslot(i % WS, slice(None)),
                             h * R_UNITS + i)

            def cut_lo(slot, dst, m):
                pool.wait_ge(unit_hi_scalar, m + 1)
                pool.tensor_tensor(dst[1], w_raw[:, slot, :], dst[0].bitcast(f32), ALU.subtract).then_inc(unit_split, 1)

            def cut_first_output(phase, u, wait, halves=(0, 1)):
                pool.wait_ge(*wait)
                cut_unit(u % RAW, loads_before(phase, u % RAW) + 16 * (u // RAW + 1), output_slot(phase, 0, u),
                         BASE[phase][0] + u, halves)

            def cut_outputs(phase, groups):
                m0 = scalar_units[0]
                for u in range(4):
                    cut_lo(u % RAW, output_slot(phase, 1, u), m0 + u)
                with pool.Fori(1, groups // 2) as i:
                    for par in range(2):
                        for u in range(4):
                            cut_lo(u % RAW, output_slot(phase, par, u),
                                   i * (2 * G_UNITS) + (m0 + G_UNITS * (par - 1) + u))
                scalar_units[0] += (groups - 1) * G_UNITS

            def add_residual(e, between):
                for tb in range(TB):
                    s = tb % 3
                    pool.wait_ge(x_loaded[s], 16 * (e * (3, 3, 2)[s] + tb // 3 + 1))
                    pool.wait_ge(z_ready, (e - 1) * TB + tb + 1)
                    for cols in residual_parts(e, tb):
                        pool.tensor_tensor(xt[:, s, cols], xt[:, s, cols], y[:, tb, cols], ALU.add).then_inc(x_new, 1)
                    if tb in between:
                        between[tb]()

            def cut_mlp(phase, e):
                n0, p0, _, o0, _ = BASE[phase]
                loaded0 = [loads_before(phase, u) for u in range(RAW)]

                def first(u):
                    pool.wait_ge(out_done, CR + o0 - 2 * LONE)
                    cut_unit(u, loaded0[u] + 16, wslot(u, slice(None)), n0 + u)
                add_residual(e, {3: lambda: first(0), 5: lambda: first(1)})
                pool.wait_ge(out_done, CR + o0)
                for u in range(2):
                    cut_unit(u, loaded0[u] + 32, wslot(2 + u, slice(None)), n0 + 2 + u)
                pool.wait_ge(proj_done, CR + p0 + M_PROJ)
                for u in range(2):
                    cut_unit(u, loaded0[u] + 48, wslot(u, slice(None)), n0 + 4 + u)
                with pool.Fori(1, N_M - 1) as g:
                    for u in range(2):
                        pool.wait_ge(proj_done, g * M_PROJ + (CR + p0 + 3 + u))
                        cut_unit(u, g * 32 + (loaded0[u] + 32), wslot(2 + u, slice(None)), g * G_UNITS + (n0 + 2 + u))
                    for u in range(2):
                        pool.wait_ge(out_done, g * G_OUT + (CR + o0))
                        cut_unit(u, g * 32 + (loaded0[u] + 48), wslot(u, slice(None)), g * G_UNITS + (n0 + 4 + u))
                g = N_M - 1
                for u in range(2):
                    pool.wait_ge(proj_done, CR + p0 + g * M_PROJ + 3 + u)
                    cut_unit(u, loaded0[u] + 32 + 32 * g, wslot(2 + u, slice(None)), n0 + 2 + g * G_UNITS + u)

            p_end = CR + RH * R_PROJ
            scores_read = (score_done, CR + BASE["R"][2] + RH * R_SCORE - 1)
            for u, wait in enumerate([scores_read, scores_read, (proj_done, p_end - 3), (proj_done, p_end - 2)]):
                cut_first_output("O0", u, wait)
            cut_outputs("O0", N_O0)
            cut_mlp("M0", 1)

            n0, p0, s0, o0, _ = BASE["A"]
            loaded0 = loads_before("A", 0)
            v_read = CR + p0 + V_PROJ
            scores_read = (score_done, CR + s0 + 2 * A_SCORE)

            def cut_v(u):
                pool.wait_ge(out_done, CR + o0 - 2 * LONE)
                cut_unit(u, loaded0 + 16, wslot(u, slice(None)), n0 + u)

            def cut_q(gp, j, halves=(0, 1)):
                if gp:
                    pool.wait_ge(proj_done, v_read + QK_PROJ)
                elif j < 2:
                    pool.wait_ge(out_done, CR + o0)
                else:
                    pool.wait_ge(proj_done, v_read)
                cut_unit(j % RAW, loaded0 + 16 + (80, 64)[j % RAW] * gp + 32 * (j // RAW + 1),
                         wslot((j + 2) % WS, slice(None)), n0 + V_UNITS + gp * A_UNITS + j, halves)
            add_residual(2, {3: lambda: cut_v(0), 5: lambda: cut_v(1)})
            for gp in range(2):
                if gp == 0:
                    for j in range(4):
                        cut_q(0, j)
                pool.wait_ge(proj_done, v_read + gp * A_PROJ + 2)
                cut_unit(0, loaded0 + 16 + 80 * gp + 80, wslot(2, slice(None)), n0 + V_UNITS + gp * A_UNITS + 4)
                for c in range(A_CORE):
                    if gp == 1 and c == A_CORE - 1:
                        cut_first_output("O1", 2, scores_read, (0,))
                    nk = len(A_BLOCKS[c // 2]) * P
                    pool.wait_ge(inv_ready, gp * A_CORE + c + 1)
                    s = a_s[:, c % 4, :, 1:1 + nk]
                    pool.tensor_tensor(s, s, row_inv[:, c % 2, :].unsqueeze(2).broadcast_to([P, 4, nk]), ALU.mult) \
                        .then_inc(p_ready, 1)
                    if gp == 0 and c >= A_CORE - 8:
                        cut_q(1, (c - (A_CORE - 8)) // 2, (c % 2,))
                    if gp == 1 and 4 <= c < 8:
                        cut_first_output("O1", (c - 4) // 2, (proj_done, v_read + A_PROJ + QK_PROJ), (c % 2,))
            cut_first_output("O1", 2, scores_read, (1,))
            cut_first_output("O1", 3, scores_read)
            cut_outputs("O1", N_O1)
            cut_mlp("M1", 3)
            add_residual(4, {})

        @block.tensor
        def _(pe):
            def mm3(dst, stat, mov, first, last):
                pe.matmul(dst, stat[0], mov[0], start=first, stop=False)
                pe.matmul(dst, stat[0], mov[1], start=False, stop=False)
                return pe.matmul(dst, stat[1], mov[0], start=False, stop=last)

            def unit_ready(n):
                pe.wait_ge(unit_split, n + (CR + 1))

            def transpose_norm(phase, tb):
                s0 = BASE[phase][2]
                pe.wait_ge(xn_ready, int(phase[1]) * TB + tb + 1)
                ring = norm_banks(phase)
                for j in range(2 * tb, 2 * tb + 2):
                    pe.wait_ge(score_free, CR + s0 + j + 1 - len(ring))
                    for k in range(4):
                        mm = pe.transpose(ring[j % len(ring)][:, part(k)], xn[:, tb % 2, part(4 * (j % 2) + k)],
                                          ident[:, :])
                    mm.then_inc(score_done, 1)

            def hT_ready(phase, blocks=TB):
                pe.wait_ge(score_free, CR + BASE[phase][2] + 2 * blocks)

            def project(slot, th, bank, free):
                pe.wait_ge(proj_free, free)
                for k in range(KT):
                    mm = mm3(proj_bank[bank][:, :], wslot(slot, part(k)), cut(hT, k, part(th, HALF)),
                             k == 0, k == KT - 1)
                mm.then_inc(proj_done, 1)

            pe.wait_ge(consts, FIRST_CONSTS)
            for tb in range(TB):
                transpose_norm("E0", tb)
            hT_ready("E0")

            _, p0, s0, o0, _ = BASE["R"]
            with pe.Fori(0, RH) as h:
                n, pj, sj = h * R_UNITS, h * R_PROJ + (CR + p0), h * R_SCORE + (CR + s0)
                for i in range(4):
                    unit_ready(n + i)
                    for th in range(2):
                        project(i, th, th, pj + (2 * i + th - 1))
                def project_v(b):
                    pe.wait_ge(proj_free, pj + (8 + b - 1))
                    for k in range(KT):
                        if b == 0 and k % 2 == 0:
                            unit_ready(n + (4 + k // 2))
                        mm = mm3(proj_bank[b % 2][:, :], cut(hT, k, part(b)), wslot(k // 2, part(k % 2, HALF)),
                                 k == 0, k == KT - 1)
                    mm.then_inc(proj_done, 1)
                for th in range(2):
                    def scores(b, th=th):
                        j = 9 * th + b
                        if th == 0 and b == 0:
                            pe.wait_ge(proj_free, pj + 8)
                        pe.wait_ge(score_free, sj + (j - 1))
                        for k in range(2):
                            mm = mm3(score_bank[j % 2][:, :], cut(r_kT, k, part(b)), cut(r_qT, k, part(th, HALF)),
                                     k == 0, k == 1)
                        mm.then_inc(score_done, 1)

                    def values(b):
                        if th == 0 and b == 0:
                            pe.wait_ge(proj_free, pj + 16)
                        pe.wait_ge(aT_ready, h * 16 + (CR + 8 * th + b + 1))
                        for dt in range(4):
                            if b == 0:
                                pe.wait_ge(out_free, h * 8 + (CR + o0 + 4 * th + dt - 3))
                            mm = mm3(out_bank[dt][:, :], cut(r_v, b, part(dt)), cut(r_aT, b % 2), b == 0, b == TB - 1)
                            if b == TB - 1:
                                mm.then_inc(out_done, 1)
                        if b < TB - 1:
                            mm.then_inc(pv_done, 1)
                    if th == 0:
                        for b in range(TB - 1):
                            project_v(b)
                        scores(0)
                        project_v(TB - 1)
                    for b in range(TB):
                        if b + 1 < TB:
                            scores(b + 1)
                        values(b)

                    def gate(dt):
                        i = 8 + 4 * th + dt
                        unit_ready(n + i)
                        project(i % WS, th, dt % 2, pj + (16 + 4 * th + dt - 1))
                    gate(0)
                    j = 9 * th + 8
                    pe.wait_ge(sq_sum, h * 2 + (th + 1))
                    pe.wait_ge(score_free, sj + (j - 1))
                    pe.matmul(score_bank[j % 2][:, :], ones[:, :], r_am[:, 0, :], start=True, stop=True) \
                      .then_inc(score_done, 1)
                    for dt in range(1, 4):
                        if th == 0 and dt == 3:
                            scores(0, th=1)
                        gate(dt)

            def out_tile(parts, first_job, j, tb, begin=True, end=True):
                if begin:
                    pe.wait_ge(out_free, first_job + (j - 3))
                for i, (par, slot) in enumerate(parts):
                    for k in range(2):
                        mm = mm3(out_bank[j % 4][:, :], cut(aT, par, k, part(tb)), wslot(slot + k, part(j % 2, HALF)),
                                 begin and i + k == 0, end and k == 1 and i == len(parts) - 1)
                if end:
                    mm.then_inc(out_done, 1)

            def out_group(par, slot, first_job):
                for j in range(G_OUT):
                    out_tile([(par, slot)], first_job, j, j // 2)

            def tail(phase, first_job, last_ready, jobs):
                more = phase != "E4"
                for j in range(2 * LONE):
                    out_tile([(0, 0)], first_job, j, TB - LONE + j // 2)
                for j in range(4):
                    out_tile([(0, 0)], first_job, 2 * LONE + j, j // 2, end=False)
                last_ready()
                for j in range(4):
                    out_tile([(1, 2)], first_job, 2 * LONE + j, j // 2, begin=False)
                for tb in range(2, TB):
                    parts = [(0, 0), (1, 2)] if tb < TB - LONE else [(1, 2)]
                    out_tile(parts, first_job, 2 * (LONE + tb), tb)
                    if more and tb >= 3:
                        transpose_norm(phase, tb - 3)
                    out_tile(parts, first_job, 2 * (LONE + tb) + 1, tb)
                if more:
                    jobs[0]()
                    transpose_norm(phase, TB - 3)
                    transpose_norm(phase, TB - 2)
                    jobs[1]()
                    transpose_norm(phase, TB - 1)
                    for job in jobs[2:]:
                        job()

            def outputs(phase, groups, after, jobs):
                n0, _, _, o0, _ = BASE[phase]
                with pe.Fori(0, groups // 2 - 1) as i:
                    for par in range(2):
                        unit_ready(i * (2 * G_UNITS) + (n0 + G_UNITS * par + 3))
                        out_group(par, 2 * par, i * (2 * G_OUT) + (CR + o0 + G_OUT * par))
                unit_ready(n0 + G_UNITS * (groups - 2) + 3)
                tail(after, CR + o0 + G_OUT * (groups - 2), lambda: unit_ready(n0 + G_UNITS * (groups - 1) + 3), jobs)

            def first_hidden(phase):
                n0, p0 = BASE[phase][:2]

                def job(u):
                    hT_ready("E" + {"M0": "1", "M1": "3"}[phase], 4)
                    unit_ready(n0 + u)
                    project(u, 0, u, CR + p0 + u - 1)
                return [lambda: job(0), lambda: job(1)]

            def mlp(phase, after, jobs):
                n0, p0, _, o0, f0 = BASE[phase]

                def up(g, slot, unit, halves=(0, 1)):
                    for th in halves:
                        for u in range(2):
                            if th == 0:
                                unit_ready(unit + u)
                            project(slot + u, th, u, g * M_PROJ + (CR + p0 + 2 * th + u - 1))

                def ready(g, unit):
                    unit_ready(unit)
                    pe.wait_ge(ff_ready, g * M_PROJ + (f0 + M_PROJ))
                up(0, 0, n0, halves=(1,))
                with pe.Fori(0, N_M // 2 - 1) as i:
                    for par in range(2):
                        g = i * 2 + par
                        up(g + 1, 2, g * G_UNITS + (n0 + 2))
                        ready(g, g * G_UNITS + (n0 + 5))
                        out_group(par, 0, g * G_OUT + (CR + o0))
                g = N_M - 2
                up(g + 1, 2, n0 + 2 + g * G_UNITS)
                ready(g, n0 + 5 + g * G_UNITS)
                tail(after, CR + o0 + g * G_OUT, lambda: ready(g + 1, n0 + 3 + (g + 1) * G_UNITS), jobs)

            outputs("O0", N_O0, "E1", first_hidden("M0"))
            hT_ready("E1")

            n0, p0, s0, _, _ = BASE["A"]

            def project_v(g):
                hT_ready("E2", 2 * g + 2)
                unit_ready(n0 + 1)
                pe.wait_ge(proj_free, CR + p0 + g - 1)
                for i in range(2):
                    for k in range(KT):
                        mm = mm3(proj_bank[g % 2][:, part(i, AG * HD)], cut(hT, k, part(2 * g + i)),
                                 wslot(k // 4, part(k % 4, AG * HD)), k == 0, k == KT - 1)
                mm.then_inc(proj_done, 1)
            mlp("M0", "E2", [lambda g=g: project_v(g) for g in range(V_PROJ)])
            hT_ready("E2")

            with pe.Fori(0, 2) as gp:
                n, pj, sj = gp * A_UNITS + (n0 + V_UNITS), gp * A_PROJ + (CR + p0 + V_PROJ), gp * A_SCORE + (CR + s0)
                for i in range(5):
                    unit_ready(n + i)
                    for th in range(2):
                        project((i + 2) % WS, th, th, pj + (2 * i + th - 1))
                pe.wait_ge(proj_free, pj + QK_PROJ - 1)
                starts = [sum(len(A_BLOCKS[c // 2]) for c in range(r)) for r in range(A_CORE)]

                def scores(c, head):
                    b, two = c // 2, c % 2
                    blocks, j = A_BLOCKS[b], 4 * c + head
                    rows = slice(HD * two, HD * two + HD)
                    pe.wait_ge(score_free, sj + (j - 3))
                    q = [t[rows, head, part(b)] for t in a_qT]
                    k = [t[rows, blocks[0] * P:(blocks[-1] + 1) * P] for t in a_kT]
                    mm3(attn_score_bank[j % 4][:, 0:len(blocks) * P], q, k, True, True).then_inc(score_done, 1)

                def turn(c, i):
                    if i == 0:
                        pe.wait_ge(p_ready, gp * A_CORE + (CR + c + 1))
                    j = QK_PROJ + starts[c] + i
                    pe.wait_ge(proj_free, pj + (j - 1))
                    for head in range(4):
                        mm = pe.transpose(proj_bank[j % 2][:, part(head)],
                                          a_s[:, c % 4, head, 1 + i * P:1 + (i + 1) * P], ident[:, :])
                    mm.then_inc(proj_done, 1)

                def values(c, i):
                    blocks, d = A_BLOCKS[c // 2], starts[c] + i
                    if i == 0:
                        pe.wait_ge(attn_free, gp * A_CORE + (CR + c - 1))
                    pe.wait_ge(proj_free, pj + (QK_PROJ + d + 1))
                    mm3(out_bank[c % 2][:, :], cut(a_v, blocks[i], slice(None)), cut(a_pT, d % A_PT_SLOTS),
                        i == 0, i == len(blocks) - 1).then_inc(attn_done, 1)

                for st in range(A_CORE + 4):
                    for what, i in (("t", 0), ("s", 0), ("s", 1), ("v", 0), ("t", 1), ("s", 2), ("v", 1), ("t", 2),
                                    ("s", 3), ("v", 2)):
                        c = st - {"s": 0, "t": 3, "v": 4}[what]
                        if 0 <= c < A_CORE and (what == "s" or i < len(A_BLOCKS[c // 2])):
                            {"s": scores, "t": turn, "v": values}[what](c, i)

            pe.wait_ge(attn_free, CR + 2 * A_CORE)
            outputs("O1", N_O1, "E3", first_hidden("M1"))
            hT_ready("E3")
            mlp("M1", "E4", [])

        @block.scalar
        def _(act):
            step = Steps(act, act_step)
            x_loads, x_stores = [0] * 3, [0] * 3


            def load_x(e, tb):
                s = tb % 3
                if x_stores[s]:
                    act.wait_ge(x_stored[s], 16 * x_stores[s])
                act.dma_start(xt[:, s, :], x_in[e][part(tb), :]).then_inc(x_loaded[s], 16)
                x_loads[s] += 1

            def norm(e, after_hi={}):
                phase = f"E{e}"
                s0, o0 = BASE[phase][2], BASE[phase][3]
                load_x(e, 0)
                for i, g in enumerate((post[e], pre[e])):
                    if g is not None:
                        act.dma_start((gain_post, gain_pre)[i][:, :], g.partition_broadcast(P)) \
                           .then_inc(gains_loaded, 16)
                load_x(e, 1)
                if e == 0:
                    act.dma_start(decay[:, 0, :], log_decay_fwd[0].partition_broadcast(P)).then_inc(params, 16)
                    act.dma_start(decay[:, 1, :], log_decay_bwd[0].partition_broadcast(P)).then_inc(params, 16)
                    act.dma_start(sink[:, :], sink_logits[0].partition_broadcast(P)).then_inc(params, 16)
                if e == 0:
                    act.wait_ge(consts, FIRST_CONSTS)
                act.activation(table_load[:, :], eps_t[:, :], ACT.Sqrt)
                banks_T = norm_banks(phase)

                def hi_part(tb):
                    for j in range(2 * tb, 2 * tb + 2):
                        act.wait_ge(score_done, CR + s0 + j + 1)
                        act.activation(hT[0][:, 4 * (j % 2):4 * (j % 2) + 4, part(tb)],
                                       banks_T[j % len(banks_T)][:, :].rearrange("p (k t) -> p k t", k=4), ACT.Copy) \
                           .then_inc(hT_hi_ready, 1)
                for st in range(TB + 3):
                    tb = st - 3
                    if 0 < e < 4 and 0 <= tb < TB:
                        hi_part(tb)
                        if tb in after_hi:
                            after_hi[tb]()
                    tb = st
                    if e and tb < TB:
                        act.wait_ge(out_free, CR + o0 - 16 + 2 * (tb + 1))
                        step(act.activation(squares, y[:, tb, :], ACT.Square, scale=D ** -0.5,
                                            accum_out=stats[:, 0, tb:tb + 1]))
                        act.activation(stats[:, 1, tb:tb + 1], stats[:, 0, tb:tb + 1], ACT.Sqrt, bias=eps_t[:, :]) \
                           .then_inc(std_y, 1)
                    tb = st - 1
                    if 0 <= tb < TB:
                        if e:
                            for i, cols in enumerate(residual_parts(e, tb)):
                                act.wait_ge(x_new, (e - 1) * TB + tb + 1 + i)
                                act.dma_start(x_out[e][part(tb), cols], xt[:, tb % 3, cols]) \
                                   .then_inc(x_stored[tb % 3], 16)
                                x_stores[tb % 3] += 1
                        else:
                            act.wait_ge(x_loaded[tb % 3], 16 * (tb // 3 + 1))
                        if e < 4:
                            step(act.activation(squares, xt[:, tb % 3, :], ACT.Square, scale=D ** -0.5,
                                                accum_out=stats[:, 2, tb:tb + 1]))
                            act.activation(stats[:, 3, tb:tb + 1], stats[:, 2, tb:tb + 1], ACT.Sqrt, bias=eps_t[:, :]) \
                               .then_inc(std_x, 1)
                    if 1 <= st < TB - 1:
                        if e < 4 and st >= 2:
                            act.wait_ge(xn_ready, e * TB + st - 1)
                        load_x(e, st + 1)
                    if e == 0 and 0 <= st - 2 < TB:
                        hi_part(st - 2)
                if e:
                    for s in range(3):
                        act.wait_ge(x_stored[s], 16 * x_stores[s])

            norm(0)

            _, p0, s0, o0, _ = BASE["R"]
            with act.Fori(0, RH) as h:
                pj, sj = h * R_PROJ + (CR + p0), h * R_SCORE + (CR + s0)

                def hi(j, dst, scale=1.0):
                    act.wait_ge(proj_done, pj + (j + 1))
                    act.activation(dst, proj_bank[j % 2][:, :], ACT.Copy, scale=scale).then_inc(proj_hi, 1)
                for j in range(8):
                    dst, u, th = (r_qT, r_kT)[j // 4], j // 2 % 2, j % 2
                    hi(j, dst[0][:, u, part(th, HALF)], 1.0 if j < 4 else DK ** -0.5)
                def masked_hi(th, b):
                    act.wait_ge(score_free, sj + (9 * th + b + 1))
                    if b >= 2:
                        act.wait_ge(pv_done, h * 14 + (CR + 7 * th + b - 1))
                    else:
                        act.wait_ge(out_done, h * 8 + (CR + 4 * th))
                    act.activation(r_aT[0][:, b % 2, :], r_am[:, b % 2, :], ACT.Copy).then_inc(aT_hi_ready, 1)
                for b in range(TB):
                    if b == TB - 1:
                        masked_hi(0, 0)
                    hi(8 + b, r_v[0][:, b, :])
                    if b == 1:
                        act.wait_ge(mask_ready, h * 4 + 4)
                        act.activation(mask[:, :], mask[:, :], ACT.Exp).then_inc(mask_exp, 1)
                for th in range(2):
                    for b in range(1, TB):
                        masked_hi(th, b)
                    act.wait_ge(aT_ready, h * 16 + (CR + 8 * th + 8))
                    for dt, dst in enumerate((r_am[:, 0, :], r_am[:, 1, :], r_e[:, :], r_sd[:, :])):
                        act.wait_ge(out_done, h * 8 + (CR + 4 * th + dt + 1))
                        act.activation(dst, out_bank[dt][:, :], ACT.Square).then_inc(sq_out, 1)
                    for dt in range(4):
                        act.wait_ge(mix_stored[dt], h * 32 + (16 + 16 * th))
                        act.activation(r_os[:, dt, :], out_bank[dt][:, :], ACT.Copy).then_inc(out_free, 1)
                    for dt in range(4):
                        if th == 0 and dt == 3:
                            masked_hi(1, 0)
                        j = 16 + 4 * th + dt
                        if dt == 0:
                            act.wait_ge(sq_sum, h * 2 + (th + 1))
                        act.wait_ge(proj_done, pj + (j + 1))
                        act.activation(r_e[:, :], proj_bank[j % 2][:, :], ACT.Sigmoid).then_inc(e_ready, 1)
                        if dt == 0:
                            act.wait_ge(score_done, sj + (9 * th + 9))
                            act.activation(r_sd[:, :], score_bank[(9 * th + 8) % 2][:, :], ACT.Sqrt, bias=eps_t[:, :],
                                           scale=1.0 / DV).then_inc(score_free, 1)
                        act.wait_ge(gated, h * 8 + (4 * th + dt + 1))
                        act.dma_start(mix[bass.ds(h * DV + dt * P, P), part(th, HALF)], r_os[:, dt, :]) \
                           .then_inc(mix_stored[dt], 16)

            def mlp(phase):
                _, p0, _, o0, f0 = BASE[phase]

                def group(g, par):
                    for j in range(4):
                        th, u = j // 2, j % 2
                        act.wait_ge(sq_ready, g * M_PROJ + (f0 + CR + j - 1))
                        act.wait_ge(proj_done, g * M_PROJ + (CR + p0 + j + 1))
                        act.activation(relu[:, j % 2, :], proj_bank[j % 2][:, :], ACT.Relu).then_inc(proj_free, 1)
                        if j == 0:
                            act.wait_ge(out_done, g * G_OUT + (CR + o0 - G_OUT))
                        act.wait_ge(proj_free, g * M_PROJ + (CR + p0 + j + 1))
                        act.activation(aT[0][:, par, u, part(th, HALF)], relu[:, j % 2, :], ACT.Square) \
                           .then_inc(ff_hi, 1)
                group(0, 0)
                with act.Fori(0, N_M // 2 - 1) as i:
                    group(i * 2 + 1, 1)
                    group(i * 2 + 2, 0)
                group(N_M - 1, 1)

            def cut_hi(phase, groups, first_waits):
                n0, _, _, o0, _ = BASE[phase]

                def unit(i, par, u):
                    act.wait_ge(raw_loaded[u % RAW],
                                i * 64 + (loads_before(phase, u % RAW) + 32 * par + 16 * (u // RAW + 1)))
                    act.activation(output_slot(phase, par, u)[0], w_raw[:, u % RAW, :], ACT.Copy) \
                       .then_inc(unit_hi_scalar, 1)
                for u in range(4):
                    act.wait_ge(*first_waits[u])
                    unit(0, 1, u)
                with act.Fori(1, groups // 2) as i:
                    for par in range(2):
                        act.wait_ge(out_done, i * (2 * G_OUT) + (CR + o0 + G_OUT * (par - 1)))
                        for u in range(4):
                            unit(i, par, u)

            p_end = CR + RH * R_PROJ
            scores_read = (score_done, CR + BASE["R"][2] + RH * R_SCORE - 1)
            cut_hi("O0", N_O0, [scores_read, scores_read, (proj_done, p_end - 1), (proj_done, p_end)])
            norm(1)
            mlp("M0")
            _, p0, s0, _, _ = BASE["A"]

            def copy_v(g):
                act.wait_ge(proj_done, CR + p0 + g + 1)
                act.activation(a_vraw[:, 2 * g:2 * g + 2, :], proj_bank[g % 2][:, :].rearrange("p (b c) -> p b c", b=2),
                               ACT.Copy).then_inc(proj_free, 1)
            norm(2, {TB - 3: lambda: copy_v(0), TB - 1: lambda: copy_v(1)})
            copy_v(2)
            copy_v(3)
            act.wait_ge(proj_free, CR + p0 + V_PROJ)

            with act.Fori(0, 2) as gp:
                pj, cj = gp * A_PROJ + (CR + p0 + V_PROJ), gp * A_CORE
                for j in range(QK_PROJ):
                    act.wait_ge(proj_done, pj + (j + 1))
                    src = proj_bank[j % 2]
                    if j < 8:
                        if j == 0:
                            act.wait_ge(scales_ready, gp + 1)
                        act.activation(a_qT[0][:, j // 2, part(j % 2, HALF)], src[:, :], ACT.Copy,
                                       scale=q_scale_now[:, j // 2:j // 2 + 1]) \
                           .then_inc(proj_hi, 1)
                    else:
                        act.activation(a_kT[0][:, part(j % 2, HALF)], src[:, :], ACT.Copy).then_inc(proj_hi, 1)
                    if j == 0:
                        act.activation(a_v[0][:, :, :], a_vraw[:, :, bass.ds(gp * P, P)], ACT.Copy)
                done = 0
                ends = [0]
                for st in range(A_CORE + 5):
                    for i in range(4):
                        c = st - 3
                        if 0 <= c < A_CORE and i < len(A_BLOCKS[c // 2]):
                            j = QK_PROJ + done
                            act.wait_ge(attn_done, gp * A_PT + (CR + done - A_PT_SLOTS + 1))
                            act.wait_ge(proj_done, pj + (j + 1))
                            act.activation(a_pT[0][:, done % A_PT_SLOTS, :], proj_bank[j % 2][:, :], ACT.Copy) \
                               .then_inc(proj_hi, 1)
                            done += 1
                            if i == len(A_BLOCKS[c // 2]) - 1:
                                ends.append(done)
                        c = st - 5
                        if 0 <= c < A_CORE and i == 0:
                            b, two = c // 2, c % 2
                            rows = slice(HD * two, HD * two + HD)
                            act.wait_ge(attn_done, gp * A_PT + (CR + ends[c + 1]))
                            act.wait_ge(attn_out[c % 2], gp * (8 * A_CORE) + 16 * (1 + c // 2))
                            act.activation(a_out[rows, :], out_bank[c % 2][rows, :], ACT.Copy) \
                               .then_inc(attn_free, 1)
                            act.wait_ge(attn_free, cj + (CR + c + 1))
                            act.dma_start(mix[bass.ds(gp * (8 * HD) + 4 * HD * two, 4 * HD), part(b)]
                                          .rearrange("(j d) t -> d j t", d=HD),
                                          a_out[rows, :].rearrange("d (j t) -> d j t", j=4)) \
                               .then_inc(attn_out[c % 2], 16)
                        c = st - 1
                        if 0 <= c < A_CORE:
                            if i == 0:
                                act.wait_ge(max_ready, cj + (c + 1))
                            s = a_s[:, c % 4, i, 0:1 + len(A_BLOCKS[c // 2]) * P]
                            ins = act.activation(s, s, ACT.Exp, bias=nmax[:, c % 2, i:i + 1],
                                                 accum_out=row_sum[:, c % 2, i:i + 1])
                            if i == 3:
                                ins.then_inc(exp_ready, 1)
            for s in attn_out:
                act.wait_ge(s, ATTN_STORES)
            q_read = (proj_done, CR + p0 + V_PROJ + A_PROJ + QK_PROJ)
            scores_read = (score_done, CR + s0 + 2 * A_SCORE)
            cut_hi("O1", N_O1, [q_read, q_read, scores_read, scores_read])
            norm(3)
            mlp("M1")
            norm(4)

        @block.vector
        def _(dve):
            step = Steps(dve, dve_step)
            gains = [0]

            def minus(dst, src, hi, scale=None):
                if scale is None:
                    return dve.tensor_tensor(dst, src, hi.bitcast(f32), ALU.subtract)
                return dve.scalar_tensor_tensor(out=dst, in0=src, scalar=scale, in1=hi.bitcast(f32), op0=ALU.mult,
                                                op1=ALU.subtract)

            def add_tile(first_job, j, tb, first=False):
                dst, src = y[:, tb, part(j % 2, HALF)], out_bank[j % 4][:, :]
                dve.wait_ge(out_done, first_job + (j + 1))
                if first:
                    dve.tensor_copy(dst, src).then_inc(out_free, 1)
                else:
                    dve.tensor_tensor(dst, dst, src, ALU.add).then_inc(out_free, 1)

            def add_group(first_job, first=False):
                dve.wait_ge(out_free, first_job)
                for j in range(G_OUT):
                    add_tile(first_job, j, j // 2, first)

            def norm(e):
                phase = f"E{e}"
                s0, o0 = BASE[phase][2], BASE[phase][3]
                tail = CR + o0 - TAIL
                gains[0] += 16 * ((post[e] is not None) + (pre[e] is not None))
                if e:
                    dve.wait_ge(out_free, tail)
                    for j in range(2 * LONE):
                        add_tile(tail, j, TB - LONE + j // 2)
                    dve.wait_ge(out_free, tail + 2 * LONE)
                banks_T = norm_banks(phase)

                def lo_part(tb):
                    for j in range(2 * tb, 2 * tb + 2):
                        dve.wait_ge(hT_hi_ready, e * 2 * TB + j + 1)
                        four = slice(4 * (j % 2), 4 * (j % 2) + 4)
                        minus(hT[1][:, four, part(tb)],
                              banks_T[j % len(banks_T)][:, :].rearrange("p (k t) -> p k t", k=4),
                              hT[0][:, four, part(tb)]).then_inc(score_free, 1)
                for st in range(TB + 3):
                    tb = st
                    if e and tb < TB:
                        add_tile(tail, 2 * (LONE + tb), tb)
                        add_tile(tail, 2 * (LONE + tb) + 1, tb)
                    if 0 < e < 4 and 0 <= st - 3 < TB:
                        lo_part(st - 3)
                    if e and tb < TB:
                        dve.wait_ge(std_y, (e - 1) * TB + tb + 1)
                        step(dve.reciprocal(stats[:, 4, tb:tb + 1], stats[:, 1, tb:tb + 1]))
                        if tb == 0:
                            dve.wait_ge(gains_loaded, gains[0])
                        dve.scalar_tensor_tensor(out=y[:, tb, :], in0=y[:, tb, :], scalar=stats[:, 4, tb:tb + 1],
                                                 in1=gain_post[:, :], op0=ALU.mult, op1=ALU.mult).then_inc(z_ready, 1)
                    tb = st - 1
                    if e < 4 and 0 <= tb < TB:
                        dve.wait_ge(std_x, e * TB + tb + 1)
                        step(dve.reciprocal(stats[:, 5, tb:tb + 1], stats[:, 3, tb:tb + 1]))
                        if e == 0 and tb == 0:
                            dve.wait_ge(gains_loaded, gains[0])
                        dve.scalar_tensor_tensor(out=xn[:, tb % 2, :], in0=xt[:, tb % 3, :],
                                                 scalar=stats[:, 5, tb:tb + 1], in1=gain_pre[:, :], op0=ALU.mult,
                                                 op1=ALU.mult).then_inc(xn_ready, 1)
                    if e == 0 and 0 <= st - 2 < TB:
                        lo_part(st - 2)

            norm(0)
            dve.wait_ge(consts, ALL_CONSTS)
            dve.tensor_copy(dist16[:, :], dist_i[:, :])
            dve.wait_ge(params, 48)
            step(dve.tensor_scalar(decay[:, 1, :], decay[:, 1, :], -1.0, None, ALU.mult))

            _, p0, s0, o0, _ = BASE["R"]
            PIECE = MASK // 4
            with dve.Fori(0, RH) as h:
                step.enter(h, 1 + 4 + 2 * (1 + 1 + 4))
                pj, sj = h * R_PROJ + (CR + p0), h * R_SCORE + (CR + s0)
                step(dve.tensor_copy(decay_now[:, :].unsqueeze(2), decay[:, :, bass.ds(h, 1)]))
                for j in range(8):
                    pair, u, th = (r_qT, r_kT)[j // 4], j // 2 % 2, j % 2
                    dve.wait_ge(proj_hi, h * 16 + (j + 1))
                    dst = cut(pair, u, part(th, HALF))
                    minus(dst[1], proj_bank[j % 2][:, :], dst[0], None if j < 4 else DK ** -0.5).then_inc(proj_free, 1)
                    if j >= 4:
                        m = slice((j - 4) * PIECE, (j - 3) * PIECE)
                        tmp = r_am[:, 0, 0:PIECE]
                        dve.tensor_scalar(mask[:, m], dist16[:, m], 0.0, decay_now[:, 0:1], ALU.max, ALU.mult)
                        step(dve.tensor_scalar(tmp, dist16[:, m], 0.0, decay_now[:, 1:2], ALU.min, ALU.mult))
                        ins = dve.tensor_tensor(mask[:, m], mask[:, m], tmp, ALU.add)
                        ins.then_inc(mask_ready, 1)
                        dve.wait_ge(mask_ready, h * 4 + (j - 3))
                def masked(th, b):
                    j = 8 * th + b
                    dve.wait_ge(aT_hi_ready, h * 16 + (CR + j - 1))
                    dve.wait_ge(score_done, sj + (9 * th + b + 1))
                    at = th * HALF + (TB - 1 - b) * P
                    dve.tensor_tensor(r_am[:, b % 2, :], score_bank[(9 * th + b) % 2][:, :], mask[:, at:at + HALF],
                                      ALU.mult).then_inc(score_free, 1)
                    dve.wait_ge(aT_hi_ready, h * 16 + (CR + j + 1))
                    minus(r_aT[1][:, b % 2, :], r_am[:, b % 2, :], r_aT[0][:, b % 2, :]).then_inc(aT_ready, 1)
                for b in range(TB):
                    if b == TB - 1:
                        dve.wait_ge(mask_exp, h + 1)
                        masked(0, 0)
                    dve.wait_ge(proj_hi, h * 16 + (9 + b))
                    minus(r_v[1][:, b, :], proj_bank[b % 2][:, :], r_v[0][:, b, :]).then_inc(proj_free, 1)
                for th in range(2):
                    for b in range(1, TB):
                        masked(th, b)
                    dve.wait_ge(sq_out, h * 8 + (4 * th + 4))
                    dve.tensor_tensor(r_am[:, 0, :], r_am[:, 0, :], r_am[:, 1, :], ALU.add)
                    step(dve.tensor_tensor(r_e[:, :], r_e[:, :], r_sd[:, :], ALU.add))
                    dve.tensor_tensor(r_am[:, 0, :], r_am[:, 0, :], r_e[:, :], ALU.add).then_inc(sq_sum, 1)
                    for dt in range(4):
                        if th == 0 and dt == 3:
                            masked(1, 0)
                        j = 16 + 4 * th + dt
                        dve.wait_ge(e_ready, h * 8 + (4 * th + dt + 1))
                        dve.tensor_tensor(r_os[:, dt, :], r_os[:, dt, :], proj_bank[j % 2][:, :], ALU.mult) \
                           .then_inc(proj_free, 1)
                        if dt == 0:
                            dve.wait_ge(score_free, sj + (9 * th + 9))
                            step(dve.reciprocal(r_sd[:, :], r_sd[:, :]))
                        dve.wait_ge(proj_free, pj + (j + 1))
                        step(dve.tensor_tensor(r_os[:, dt, :], r_os[:, dt, :], r_sd[:, :], ALU.mult))
                        dve.tensor_tensor(r_os[:, dt, :], r_os[:, dt, :], r_e[:, :], ALU.mult).then_inc(gated, 1)
            step.leave(RH)

            def outputs(phase, groups):
                o0 = BASE[phase][3]
                add_group(CR + o0, first=True)
                with dve.Fori(1, groups - 2) as g:
                    add_group(g * G_OUT + (CR + o0))

            def mlp(phase):
                _, p0, _, o0, f0 = BASE[phase]

                def hidden(g, par):
                    for j in range(4):
                        th, u = j // 2, j % 2
                        dve.wait_ge(proj_free, g * M_PROJ + (CR + p0 + j + 1))
                        r = relu[:, j % 2, :]
                        dve.tensor_tensor(relu_sq[:, j % 2, :], r, r, ALU.mult).then_inc(sq_ready, 1)
                        dve.wait_ge(sq_ready, g * M_PROJ + (f0 + CR + j + 1))
                        dve.wait_ge(ff_hi, g * M_PROJ + (f0 + j + 1))
                        dst = cut(aT, par, u, part(th, HALF))
                        minus(dst[1], relu_sq[:, j % 2, :], dst[0]).then_inc(ff_ready, 1)
                hidden(0, 0)
                hidden(1, 1)
                add_group(CR + o0, first=True)
                with dve.Fori(0, N_M // 2 - 2) as i:
                    for par in range(2):
                        g = i * 2 + (1 + par)
                        hidden(g + 1, par)
                        add_group(g * G_OUT + (CR + o0))
                g = N_M - 3
                hidden(g + 1, 0)
                add_group(g * G_OUT + (CR + o0))
                hidden(g + 2, 1)

            outputs("O0", N_O0)
            norm(1)
            mlp("M0")
            norm(2)

            _, p0, s0, _, _ = BASE["A"]
            h0 = 16 * RH
            step(dve.tensor_copy(a_dist[:, :], a_iota[:, :]))
            step(dve.tensor_scalar(a_far[:, :], a_dist[:, :], -1.0, None, ALU.mult))
            step(dve.tensor_tensor(a_dist[:, :], a_dist[:, :], a_far[:, :], ALU.max))
            step(dve.tensor_scalar(a_far[:, :], a_dist[:, :], float(P), BIG, ALU.is_gt, ALU.mult))
            step(dve.tensor_tensor(a_dist[:, :], a_dist[:, :], a_far[:, :], ALU.add))
            with dve.Fori(0, 2) as gp:
                sj, cj = gp * A_SCORE + (CR + s0), gp * A_CORE
                dve.tensor_copy(slope_now[:, :], slope[:, bass.ds(gp * 8, 8)])
                dve.tensor_copy(sink_now[:, :], sink[:, bass.ds(gp * 8, 8)])
                dve.tensor_copy(q_scale_now[:, :], q_scale[:, bass.ds(gp * 4, 4)]).then_inc(scales_ready, 1)
                dve.wait_ge(scales_ready, gp + 1)
                for j in range(QK_PROJ):
                    dve.wait_ge(proj_hi, gp * A_PROJ + (h0 + j + 1))
                    src = proj_bank[j % 2]
                    if j < 8:
                        dst = cut(a_qT, j // 2, part(j % 2, HALF))
                        minus(dst[1], src[:, :], dst[0], q_scale_now[:, j // 2:j // 2 + 1]).then_inc(proj_free, 1)
                    else:
                        dst = cut(a_kT, part(j % 2, HALF))
                        minus(dst[1], src[:, :], dst[0]).then_inc(proj_free, 1)
                    if j == 1:
                        minus(a_v[1][:, :, :], a_vraw[:, :, bass.ds(gp * P, P)], a_v[0][:, :, :])
                done = 0
                for st in range(A_CORE + 3):
                    if st < A_CORE:
                        b, two = st // 2, st % 2
                        blocks = A_BLOCKS[b]
                        nk, left = len(blocks) * P, (blocks[0] - b + 1) * P
                    for head in range(4):
                        if st < A_CORE:
                            own = slice(4 * two + head, 4 * two + head + 1)
                            dve.wait_ge(score_done, sj + (4 * st + head + 1))
                            dve.tensor_copy(a_s[:, st % 4, head, 0:1], sink_now[:, own])
                            dve.tensor_tensor_reduce(out=a_s[:, st % 4, head, 1:1 + nk],
                                                     in0=attn_score_bank[head][:, 0:nk],
                                                     in1=a_dist[:, left:left + nk], scale=slope_now[:, own],
                                                     scalar=sink_now[:, own], op0=ALU.add, op1=ALU.max,
                                                     accum_out=smax[:, st % 2, head:head + 1]).then_inc(score_free, 1)
                        c = st - 3
                        if c >= 0 and head < len(A_BLOCKS[c // 2]):
                            dve.wait_ge(proj_hi, gp * A_PROJ + (h0 + QK_PROJ + done + 1))
                            dst = cut(a_pT, done % A_PT_SLOTS)
                            minus(dst[1], proj_bank[done % 2][:, :], dst[0]).then_inc(proj_free, 1)
                            done += 1
                    if st < A_CORE:
                        dve.wait_ge(score_free, sj + (4 * st + 4))
                        dve.tensor_scalar(nmax[:, st % 2, :], smax[:, st % 2, :], -1.0, None, ALU.mult) \
                           .then_inc(max_ready, 1)
                    c = st - 1
                    if 0 <= c < A_CORE:
                        dve.wait_ge(exp_ready, cj + (c + 1))
                        dve.reciprocal(row_inv[:, c % 2, :], row_sum[:, c % 2, :]).then_inc(inv_ready, 1)

            outputs("O1", N_O1)
            norm(3)
            mlp("M1")
            norm(4)


_INS = ["x", "w_in_ret", "w_out_ret", "log_decay_fwd", "log_decay_bwd", "w_in_attn", "w_out_attn", "sink_logits",
        "g_pre_mix", "g_post_mix", "g_pre_mlp", "g_post_mlp", "w_up", "w_down"]


def kernel(**inputs):
    import numpy as np
    import concourse.bacc as bacc
    from concourse.bass_utils import run_bass_kernel_spmd

    nc = bacc.Bacc("TRN2", target_bir_lowering=False, num_devices=1)
    arrays, args = {}, []
    for name in _INS:
        a = np.ascontiguousarray(inputs[name])
        arrays[f"in_{name}"] = a
        args.append(nc.dram_tensor(f"in_{name}", a.shape, mybir.dt.from_np(a.dtype), kind="ExternalInput").ap())
    args.append(nc.dram_tensor("result", (1, T, D), mybir.dt.float32, kind="ExternalOutput").ap())
    build(nc, *args)
    r = run_bass_kernel_spmd(nc, [arrays], core_ids=[0])
    return r.results[0]["result"]
```
